# Optimizing a Trainium2 kernel written in Bass

```python
import jax, jax.numpy as jnp
from jax import lax
import numpy as np

D_MODEL = 1024
BATCH = 1
SEQ = 256
DEPTH = 1

HGRN_EXPAND = 128
HGRN_WIDTH = D_MODEL
HGRN_HEADS = HGRN_WIDTH // HGRN_EXPAND
HGRN_HEAD_V = HGRN_WIDTH // HGRN_HEADS
HGRN_CHUNK = 16
POOL_WINDOWS = (2, 4, 8, 16)
POOL_GROUPS = len(POOL_WINDOWS)
POOL_WIDTH = D_MODEL
POOL_GROUP_DIM = POOL_WIDTH // POOL_GROUPS
D_FF = 4 * D_MODEL
IN_COLS = 4 * HGRN_WIDTH + POOL_WIDTH + 2 * D_MODEL
DEEPNORM_ALPHA = (2.0 * DEPTH) ** 0.25
DEEPNORM_BETA = (8.0 * DEPTH) ** -0.25
LN_EPS = 1e-5
RMS_EPS = 1e-6


def layer_norm(x, g, b):
    xf = x.astype(jnp.float32)
    mu = jnp.mean(xf, axis=-1, keepdims=True)
    var = jnp.mean(jnp.square(xf - mu), axis=-1, keepdims=True)
    y = (xf - mu) * lax.rsqrt(var + LN_EPS)
    return (y * g.astype(jnp.float32) + b.astype(jnp.float32)).astype(x.dtype)

def hgrn2_chunked(q, k, v, log_f):
    B, S, H, dk = q.shape
    dv = v.shape[-1]
    n = S // HGRN_CHUNK

    def to_chunks(t):
        return t.reshape(B, n, HGRN_CHUNK, H, t.shape[-1]).transpose(1, 0, 3, 2, 4)

    q, k, v, log_f = to_chunks(q), to_chunks(k), to_chunks(v), to_chunks(log_f)
    G = jnp.cumsum(log_f, axis=3)
    G_last = G[:, :, :, -1:, :]
    q_dec = q * jnp.exp(G)
    k_inv = k * jnp.exp(-G)
    k_to_end = k * jnp.exp(G_last - G)
    causal = jnp.tril(jnp.ones((HGRN_CHUNK, HGRN_CHUNK), dtype=bool))
    scores = jnp.einsum('nbhtd,nbhsd->nbhts', q_dec, k_inv)
    scores = jnp.where(causal, scores, 0.0)
    o_intra = jnp.einsum('nbhts,nbhsv->nbhtv', scores, v)

    def step(state, xs):
        q_c, k_c, v_c, decay_c = xs
        o_inter = jnp.einsum('bhtd,bhdv->bhtv', q_c, state)
        new_state = jnp.swapaxes(decay_c, -1, -2) * state + jnp.einsum('bhsd,bhsv->bhdv', k_c, v_c)
        return new_state, o_inter

    state0 = jnp.zeros((B, H, dk, dv), jnp.float32)
    _, o_inter = lax.scan(step, state0, (q_dec, k_to_end, v, jnp.exp(G_last)))
    o = o_intra + o_inter
    return o.transpose(1, 0, 3, 2, 4).reshape(B, S, H, dv)

def causal_multiscale_pool(v):
    B, S, _ = v.shape
    vg = v.reshape(B, S, POOL_GROUPS, POOL_GROUP_DIM).astype(jnp.float32)
    csum = jnp.cumsum(vg, axis=1)
    pos = jnp.arange(S)
    outs = []
    for g, w in enumerate(POOL_WINDOWS):
        c = csum[:, :, g]
        lagged = jnp.pad(c, ((0, 0), (w, 0), (0, 0)))[:, :S]
        count = jnp.minimum(pos + 1, w).astype(jnp.float32)[:, None]
        outs.append((c - lagged) / count - vg[:, :, g])
    return jnp.stack(outs, axis=2).astype(v.dtype)

def hybrid_mixer(x, w_in, lower_bound, hgrn_norm_g, w_a, w_pool, pool_scale, w_out):
    B, S, _ = x.shape
    proj = x @ w_in
    hw = HGRN_WIDTH
    splits = [hw, 2 * hw, 3 * hw, 4 * hw, 4 * hw + POOL_WIDTH, 4 * hw + POOL_WIDTH + D_MODEL]
    q, f_pre, i_val, o_gate, pool_v, gate_a, gate_b = jnp.split(proj, splits, axis=-1)

    qf = jax.nn.silu(q.astype(jnp.float32)) * (HGRN_EXPAND ** -0.5)
    lb = lower_bound.astype(jnp.float32)
    f = lb + (1.0 - lb) * jax.nn.sigmoid(f_pre.astype(jnp.float32))
    k = 1.0 - f
    log_f = jnp.log(f)
    shp = (B, S, HGRN_HEADS, HGRN_EXPAND)
    o = hgrn2_chunked(qf.reshape(shp), k.reshape(shp),
                      i_val.astype(jnp.float32).reshape(B, S, HGRN_HEADS, HGRN_HEAD_V), log_f.reshape(shp))
    o = o * lax.rsqrt(jnp.mean(jnp.square(o), axis=-1, keepdims=True) + RMS_EPS)
    o = o.reshape(B, S, hw) * hgrn_norm_g.astype(jnp.float32) * jax.nn.sigmoid(o_gate.astype(jnp.float32))
    a = o.astype(x.dtype) @ w_a

    pooled = causal_multiscale_pool(pool_v)
    b = jnp.einsum('bsgc,gcd->bsgd', pooled, w_pool).reshape(B, S, POOL_WIDTH) * pool_scale

    merged = jax.nn.sigmoid(gate_a) * a + jax.nn.sigmoid(gate_b) * b
    return merged @ w_out

def sq_relu_mlp(x, w_up, w_down):
    return jnp.square(jax.nn.relu(x @ w_up)) @ w_down

def first_inputs(seed: int = 0) -> dict:
    key = jax.random.key(seed)
    ks = jax.random.split(key, 15)
    f32 = jnp.float32
    nrm = lambda k, s: jax.random.normal(k, s, f32)
    return {
        "x": nrm(ks[0], (BATCH, SEQ, D_MODEL)),
        "w_in": nrm(ks[1], (DEPTH, D_MODEL, IN_COLS)) * D_MODEL ** -0.5,
        "lb_logits": nrm(ks[2], (DEPTH + 1, HGRN_WIDTH)) * 0.5,
        "hgrn_norm_g": 1.0 + 0.05 * nrm(ks[3], (DEPTH, HGRN_WIDTH)),
        "w_a": nrm(ks[4], (DEPTH, HGRN_WIDTH, D_MODEL)) * HGRN_WIDTH ** -0.5,
        "w_pool": nrm(ks[5], (DEPTH, POOL_GROUPS, POOL_GROUP_DIM, POOL_GROUP_DIM)) * POOL_GROUP_DIM ** -0.5,
        "pool_scale": 1.0 + 0.05 * nrm(ks[6], (DEPTH, POOL_WIDTH)),
        "w_out": nrm(ks[7], (DEPTH, D_MODEL, D_MODEL)) * (D_MODEL ** -0.5) * DEEPNORM_BETA,
        "ln1_g": 1.0 + 0.05 * nrm(ks[8], (DEPTH, D_MODEL)),
        "ln1_b": 0.02 * nrm(ks[9], (DEPTH, D_MODEL)),
        "w_up": nrm(ks[10], (DEPTH, D_MODEL, D_FF)) * D_MODEL ** -0.5,
        "w_down": nrm(ks[11], (DEPTH, D_FF, D_MODEL)) * (D_FF ** -0.5) * DEEPNORM_BETA,
        "ln2_g": 1.0 + 0.05 * nrm(ks[12], (DEPTH, D_MODEL)),
        "ln2_b": 0.02 * nrm(ks[13], (DEPTH, D_MODEL)),
    }

def first_block(x, w_in, lb_logits, hgrn_norm_g, w_a, w_pool, pool_scale, w_out,
              ln1_g, ln1_b, w_up, w_down, ln2_g, ln2_b):
    lower_bounds = jnp.cumsum(jax.nn.softmax(lb_logits.astype(jnp.float32), axis=0), axis=0)
    for l in range(DEPTH):
        mix = hybrid_mixer(x, w_in[l], lower_bounds[l], hgrn_norm_g[l], w_a[l], w_pool[l],
                           pool_scale[l], w_out[l])
        x = layer_norm(DEEPNORM_ALPHA * x + mix, ln1_g[l], ln1_b[l])
        x = layer_norm(DEEPNORM_ALPHA * x + sq_relu_mlp(x, w_up[l], w_down[l]), ln2_g[l], ln2_b[l])
    return x


N_MEM = 256
EPS = 1e-6
NEG = -1e30
ROPE_THETA = 10000.0
MOBA_HEADS = 8
MOBA_HD = 64
MOBA_WIDTH = MOBA_HEADS * MOBA_HD
MOBA_BLOCK = 256
MOBA_TOPK = 3
Q_CHUNK = 128
GMLP_GROUPS = 8
GMLP_GD = 64
GMLP_WIDTH = GMLP_GROUPS * GMLP_GD
GMLP_CHUNK = 128
N_BRANCH = 2
IN_COLS_2 = 3 * MOBA_WIDTH + 2 * GMLP_WIDTH + N_BRANCH * D_MODEL
XA_HEADS = 4
XA_HD = 128
XA_WIDTH = XA_HEADS * XA_HD
PEER_HEADS = 8
PEER_NKEYS = 128
PEER_N = PEER_NKEYS * PEER_NKEYS
PEER_DQ = 256
PEER_TOPK = 16
PEER_TOK_CHUNK = 128


def rmsnorm(x, g):
    xf = x.astype(jnp.float32)
    y = xf * lax.rsqrt(jnp.mean(xf * xf, axis=-1, keepdims=True) + EPS)
    return (y * g.astype(jnp.float32)).astype(x.dtype)

def rope(x):
    S, Dh = x.shape[1], x.shape[3]
    half = Dh // 2
    freqs = ROPE_THETA ** (-jnp.arange(half, dtype=jnp.float32) / half)
    ang = jnp.arange(S, dtype=jnp.float32)[:, None] * freqs[None, :]
    c = jnp.cos(ang)[None, :, None, :]
    s = jnp.sin(ang)[None, :, None, :]
    xf = x.astype(jnp.float32)
    x1, x2 = xf[..., :half], xf[..., half:]
    return jnp.concatenate([x1 * c - x2 * s, x2 * c + x1 * s], axis=-1).astype(x.dtype)

def moba_attention(q, k, v):
    B, S, H, Dh = q.shape
    nb = -(-S // MOBA_BLOCK)
    pad = nb * MOBA_BLOCK - S
    nq = S // Q_CHUNK
    top = min(MOBA_TOPK, nb)
    kp = jnp.pad(k, ((0, 0), (0, pad), (0, 0), (0, 0)))
    vp = jnp.pad(v, ((0, 0), (0, pad), (0, 0), (0, 0)))
    kb = kp.reshape(B, nb, MOBA_BLOCK, H, Dh).transpose(0, 3, 1, 2, 4)
    vb = vp.reshape(B, nb, MOBA_BLOCK, H, Dh).transpose(0, 3, 1, 2, 4)
    k_mean = jnp.mean(kb.astype(jnp.float32), axis=3)
    q_blk = jnp.arange(S) // MOBA_BLOCK
    past = jnp.arange(nb)[None, :] < q_blk[:, None]
    gate = jnp.einsum("bshd,bhnd->bhsn", q.astype(jnp.float32), k_mean)
    gate = jnp.where(past[None, None], gate, NEG)
    _, sel = lax.top_k(gate, top)
    q_c = q.reshape(B, nq, Q_CHUNK, H, Dh).transpose(0, 1, 3, 2, 4).reshape(B * nq, H, Q_CHUNK, Dh)
    sel_c = sel.reshape(B, H, nq, Q_CHUNK, top).transpose(0, 2, 1, 3, 4).reshape(B * nq, H, Q_CHUNK, top)
    scale = Dh ** -0.5
    h_idx = jnp.arange(H)[:, None, None]

    def query_block(args):
        i, qc, si = args
        b = i // nq
        c = i % nq
        kb_b = kb[b]
        vb_b = vb[b]
        pos = c * Q_CHUNK + jnp.arange(Q_CHUNK)
        valid = si < (pos // MOBA_BLOCK)[None, :, None]
        k_sel = kb_b[h_idx, si]
        v_sel = vb_b[h_idx, si]
        s_sel = jnp.einsum("hqd,hqnld->hqnl", qc, k_sel).astype(jnp.float32) * scale
        s_sel = jnp.where(valid[..., None], s_sel, NEG).reshape(H, Q_CHUNK, top * MOBA_BLOCK)
        own = (c * Q_CHUNK) // MOBA_BLOCK
        k_own = lax.dynamic_index_in_dim(kb_b, own, axis=1, keepdims=False)
        v_own = lax.dynamic_index_in_dim(vb_b, own, axis=1, keepdims=False)
        s_own = jnp.einsum("hqd,hld->hql", qc, k_own).astype(jnp.float32) * scale
        k_pos = own * MOBA_BLOCK + jnp.arange(MOBA_BLOCK)
        s_own = jnp.where((k_pos[None, :] <= pos[:, None])[None], s_own, NEG)
        p = jax.nn.softmax(jnp.concatenate([s_sel, s_own], axis=-1), axis=-1).astype(qc.dtype)
        p_sel = p[..., :top * MOBA_BLOCK].reshape(H, Q_CHUNK, top, MOBA_BLOCK)
        p_own = p[..., top * MOBA_BLOCK:]
        return (jnp.einsum("hqnl,hqnld->hqd", p_sel, v_sel)
                + jnp.einsum("hql,hld->hqd", p_own, v_own))

    out = lax.map(query_block, (jnp.arange(B * nq), q_c, sel_c))
    return out.reshape(B, nq, H, Q_CHUNK, Dh).transpose(0, 1, 3, 2, 4).reshape(B, S, H * Dh)

def gmlp_spatial_gating(u, v, norm_g, w_s, b_s):
    B, S, _ = u.shape
    nc = S // GMLP_CHUNK
    u = jax.nn.gelu(u)
    v = rmsnorm(jax.nn.gelu(v), norm_g)
    vc = v.reshape(B, nc, GMLP_CHUNK, GMLP_GROUPS, GMLP_GD)
    causal = jnp.tril(jnp.ones((GMLP_CHUNK, GMLP_CHUNK), dtype=bool))
    wm = jnp.where(causal[None], w_s, 0.0).astype(v.dtype)
    z = jnp.einsum("gts,bcsgd->bctgd", wm, vc) + b_s.T.astype(v.dtype)[None, None, :, :, None]
    return u * z.reshape(B, S, GMLP_WIDTH)

def memory_cross_attention(h, m, w_q, w_kv, w_o):
    B, S, _ = h.shape
    M = m.shape[1]
    q = (h @ w_q).reshape(B, S, XA_HEADS, XA_HD)
    k, v = jnp.split(m @ w_kv, 2, axis=-1)
    k = k.reshape(B, M, XA_HEADS, XA_HD)
    v = v.reshape(B, M, XA_HEADS, XA_HD)
    s = jnp.einsum("bshd,bmhd->bhsm", q, k).astype(jnp.float32) * (XA_HD ** -0.5)
    p = jax.nn.softmax(s, axis=-1).astype(h.dtype)
    o = jnp.einsum("bhsm,bmhd->bshd", p, v).reshape(B, S, XA_WIDTH)
    return o @ w_o

def peer_ffn(h, w_q, subkeys, w_down, w_up):
    B, S, D = h.shape
    n_chunks = (B * S) // PEER_TOK_CHUNK
    half = PEER_DQ // 2
    kk = PEER_TOPK * PEER_TOPK

    def token_chunk(xc):
        q = (xc @ w_q).reshape(PEER_TOK_CHUNK, PEER_HEADS, 2, half).astype(jnp.float32)
        s = jnp.einsum("thpd,hpnd->thpn", q, subkeys.astype(jnp.float32))
        s1, i1 = lax.top_k(s[:, :, 0], PEER_TOPK)
        s2, i2 = lax.top_k(s[:, :, 1], PEER_TOPK)
        cand_s = (s1[..., :, None] + s2[..., None, :]).reshape(PEER_TOK_CHUNK, PEER_HEADS, kk)
        cand_i = (i1[..., :, None] * PEER_NKEYS + i2[..., None, :]).reshape(PEER_TOK_CHUNK, PEER_HEADS, kk)
        top_s, top_pos = lax.top_k(cand_s, PEER_TOPK)
        e = jnp.take_along_axis(cand_i, top_pos, axis=-1)
        g = jax.nn.softmax(top_s, axis=-1).astype(xc.dtype)
        a = jax.nn.gelu(jnp.einsum("td,thkd->thk", xc, w_down[e]))
        return jnp.einsum("thk,thkd->td", g * a, w_up[e])

    y = lax.map(token_chunk, h.reshape(n_chunks, PEER_TOK_CHUNK, D))
    return y.reshape(B, S, D)

def second_inputs(seed: int = 0) -> dict:
    key = jax.random.key(seed)
    ks = jax.random.split(key, 24)

    def nrm(k, shape, scale):
        return jax.random.normal(k, shape, jnp.float32) * scale

    def gain(k, shape):
        return 1.0 + 0.01 * jax.random.normal(k, shape, jnp.float32)

    return {
        "x": nrm(ks[0], (BATCH, SEQ, D_MODEL), 1.0),
        "mem": nrm(ks[1], (BATCH, N_MEM, D_MODEL), 1.0),
        "norm_mix_g": gain(ks[2], (DEPTH, D_MODEL)),
        "w_in": nrm(ks[3], (DEPTH, D_MODEL, IN_COLS_2), D_MODEL ** -0.5),
        "moba_w_proj": nrm(ks[4], (DEPTH, MOBA_WIDTH, D_MODEL), MOBA_WIDTH ** -0.5),
        "gmlp_norm_g": gain(ks[5], (DEPTH, GMLP_WIDTH)),
        "gmlp_w_s": nrm(ks[6], (DEPTH, GMLP_GROUPS, GMLP_CHUNK, GMLP_CHUNK), GMLP_CHUNK ** -0.5),
        "gmlp_b_s": 1.0 + 0.1 * jax.random.normal(ks[7], (DEPTH, GMLP_GROUPS, GMLP_CHUNK), jnp.float32),
        "gmlp_w_proj": nrm(ks[8], (DEPTH, GMLP_WIDTH, D_MODEL), GMLP_WIDTH ** -0.5),
        "w_out": nrm(ks[9], (DEPTH, D_MODEL, D_MODEL), D_MODEL ** -0.5),
        "norm_xa_g": gain(ks[10], (DEPTH, D_MODEL)),
        "norm_mem_g": gain(ks[11], (DEPTH, D_MODEL)),
        "xa_w_q": nrm(ks[12], (DEPTH, D_MODEL, XA_WIDTH), D_MODEL ** -0.5),
        "xa_w_kv": nrm(ks[13], (DEPTH, D_MODEL, 2 * XA_WIDTH), D_MODEL ** -0.5),
        "xa_w_o": nrm(ks[14], (DEPTH, XA_WIDTH, D_MODEL), XA_WIDTH ** -0.5),
        "norm_ffn_g": gain(ks[15], (DEPTH, D_MODEL)),
        "peer_w_q": nrm(ks[16], (DEPTH, D_MODEL, PEER_HEADS * PEER_DQ), D_MODEL ** -0.5),
        "peer_subkeys": nrm(ks[17], (DEPTH, PEER_HEADS, 2, PEER_NKEYS, PEER_DQ // 2), (PEER_DQ // 2) ** -0.5),
        "peer_w_down": nrm(ks[18], (DEPTH, PEER_N, D_MODEL), D_MODEL ** -0.5),
        "peer_w_up": nrm(ks[19], (DEPTH, PEER_N, D_MODEL), 0.3),
        "final_g": gain(ks[20], (D_MODEL,)),
    }

def second_block(x, mem, norm_mix_g, w_in, moba_w_proj, gmlp_norm_g, gmlp_w_s, gmlp_b_s,
              gmlp_w_proj, w_out, norm_xa_g, norm_mem_g, xa_w_q, xa_w_kv, xa_w_o,
              norm_ffn_g, peer_w_q, peer_subkeys, peer_w_down, peer_w_up, final_g):
    B, S, _ = x.shape
    splits = list(np.cumsum([MOBA_WIDTH, MOBA_WIDTH, MOBA_WIDTH, GMLP_WIDTH, GMLP_WIDTH, D_MODEL]))
    for l in range(DEPTH):
        h = rmsnorm(x, norm_mix_g[l])
        proj = h @ w_in[l]
        q, k, v, gu, gv, gate_a, gate_b = jnp.split(proj, splits, axis=-1)
        q = rope(q.reshape(B, S, MOBA_HEADS, MOBA_HD))
        k = rope(k.reshape(B, S, MOBA_HEADS, MOBA_HD))
        v = v.reshape(B, S, MOBA_HEADS, MOBA_HD)
        y_a = moba_attention(q, k, v) @ moba_w_proj[l]
        y_b = gmlp_spatial_gating(gu, gv, gmlp_norm_g[l], gmlp_w_s[l], gmlp_b_s[l]) @ gmlp_w_proj[l]
        merged = jax.nn.sigmoid(gate_a) * y_a + jax.nn.sigmoid(gate_b) * y_b
        x = x + merged @ w_out[l]
        h = rmsnorm(x, norm_xa_g[l])
        m = rmsnorm(mem, norm_mem_g[l])
        x = x + memory_cross_attention(h, m, xa_w_q[l], xa_w_kv[l], xa_w_o[l])
        h = rmsnorm(x, norm_ffn_g[l])
        x = x + peer_ffn(h, peer_w_q[l], peer_subkeys[l], peer_w_down[l], peer_w_up[l])
    return rmsnorm(x, final_g)


def setup_inputs(seed=0):
    out = dict(first_inputs(seed))
    for name, value in second_inputs(seed + 1).items():
        if name != "x":
            out[name + "_2"] = value
    return out


def reference(
    x, w_in, lb_logits, hgrn_norm_g, w_a, w_pool, pool_scale, w_out, ln1_g, ln1_b, w_up, w_down,
    ln2_g, ln2_b, mem_2, norm_mix_g_2, w_in_2, moba_w_proj_2, gmlp_norm_g_2, gmlp_w_s_2,
    gmlp_b_s_2, gmlp_w_proj_2, w_out_2, norm_xa_g_2, norm_mem_g_2, xa_w_q_2, xa_w_kv_2,
    xa_w_o_2, norm_ffn_g_2, peer_w_q_2, peer_subkeys_2, peer_w_down_2, peer_w_up_2, final_g_2,
):
    x = first_block(
        x, w_in, lb_logits, hgrn_norm_g, w_a, w_pool, pool_scale, w_out, ln1_g, ln1_b, w_up,
        w_down, ln2_g, ln2_b,
    )
    return second_block(
        x, mem_2, norm_mix_g_2, w_in_2, moba_w_proj_2, gmlp_norm_g_2, gmlp_w_s_2, gmlp_b_s_2,
        gmlp_w_proj_2, w_out_2, norm_xa_g_2, norm_mem_g_2, xa_w_q_2, xa_w_kv_2, xa_w_o_2,
        norm_ffn_g_2, peer_w_q_2, peer_subkeys_2, peer_w_down_2, peer_w_up_2, final_g_2,
    )


_drawn_inputs = setup_inputs


def setup_inputs(seed=0):
    import zlib

    import numpy as np

    out = dict(_drawn_inputs(seed))
    spreads = {}
    factors = {'lb_logits': 3.216,
     'hgrn_norm_g': 3.805,
     'norm_mix_g_2': 4.353,
     'gmlp_norm_g_2': 6.915,
     'norm_xa_g_2': 8.0,
     'norm_mem_g_2': 8.0,
     'norm_ffn_g_2': 27.84,
     'final_g_2': 31.91}
    for name, (base, spread) in spreads.items():
        noise = np.random.default_rng([zlib.crc32(name.encode()), seed]).standard_normal(out[name].shape)
        drawn = base * np.exp(spread * noise) if base else spread * noise
        out[name] = __import__('jax').numpy.asarray(drawn.astype(out[name].dtype))
    for name, factor in factors.items():
        out[name] = (out[name] * factor).astype(out[name].dtype)
    return out
```

```python
from contextlib import ExitStack

import numpy as np
import concourse.bass as bass
import concourse.mybir as mybir

P = 128
T = 256
MT = T // P
D = 1024
DC = D // P
HEADS = 8
CH = 16
NCH = T // CH
FF = 4096
MH, MHD = 8, 64
XH, XHD = 4, 128
PH, NK, TOPK = 8, 128, 16
ALPHA = 2.0 ** 0.25
LN_EPS, RMS_EPS = 1e-5, 1e-6
NEG = -1e30
LOWEST = -3.0e38

F32 = mybir.dt.float32
U32 = mybir.dt.uint32
ALU = mybir.AluOpType
ACT = mybir.ActivationFunctionType
AX = mybir.AxisListType.X

STAGES = [
    ("f", 4, 4), ("q", 4, 4), ("i", 4, 4), ("pv", 4, 4), ("og", 4, 4), ("ga", 4, 4), ("gb", 4, 4),
    ("pool", 1, 4), ("wa", 4, 4), ("wo", 4, 4), ("xk", 2, 2), ("up", 16, 16), ("down", 16, 4),
    ("xv", 2, 2), ("q2", 2, 2), ("k2", 2, 2), ("v2", 2, 2), ("gu", 2, 2), ("gv", 2, 2),
    ("ga2", 4, 4), ("gb2", 4, 4), ("ma", 2, 4), ("gm", 2, 4), ("wo2", 4, 4), ("xq", 2, 2),
    ("xo", 2, 4), ("pq", 8, 8),
]
BLOCK, UNIT, RING = {}, {}, {}
last_unit = []
_b = _u = _r = 0
for _n, _nb, _ng in STAGES:
    BLOCK[_n], UNIT[_n], RING[_n] = _b, _u, _r
    for _i in range(_nb):
        _u += max(1, _ng // _nb)
        last_unit.append(_u - 1)
    _b, _r = _b + _nb, _r + _ng
NBLOCKS = _b

AUX = {}
_a = 0
for _n, _k in [("kT", 4), ("sc", 4), ("U", 30), ("osum", 1), ("obc", 4), ("memT", 4), ("ln1T", 4),
               ("h2T", 4), ("pv0", 1), ("pv1", 1), ("z", 2), ("h3T", 4), ("xpv", 2), ("h4T", 4),
               ("psc", 8)]:
    AUX[_n] = _a
    _a += _k

VEC = {n: 8 * i for i, n in enumerate(
    ["lb0", "lb1", "hg", "ps", "ln1g", "ln1b", "mixg", "xag", "memg"])}
NVEC = 8 * len(VEC)
CON, _c = {}, 0
for _n, _k in [("ident", 128), ("ones", 128), ("amask", 384), ("cmask", 128), ("cos", 256),
               ("sin", 256), ("invc", 64), ("reset", 256), ("even", 1), ("odd", 1), ("iota", 16),
               ("zero", 1)]:
    CON[_n] = (_c, _k)
    _c += _k
NCON = _c


class Steps:

    def __init__(self, eng, sem):
        self.eng, self.sem, self.n, self.dyn = eng, sem, 0, 0
        self.met = None

    def do(self, ins):
        ins.then_inc(self.sem, 1)
        self.n += 1

    def sync(self):
        self.wait(self.sem, self.dyn + self.n)

    def wait(self, sem, value):
        if self.met and not isinstance(value, int):
            value = self.eng.to_reg(value)
            self.eng.wait_ge(*self.met)
        self.eng.wait_ge(sem, value)

    def then(self, ins):
        self.do(ins)
        self.sync()

    def loop(self, start, end, per):
        return _Loop(self, start, end, per)


class _Loop:
    def __init__(self, steps, start, end, per):
        self.s, self.a, self.b, self.per = steps, start, end, per

    def __enter__(self):
        self.cm = self.s.eng.Fori(self.a, self.b)
        i = self.cm.__enter__()
        self.n0 = self.s.n
        self.s.dyn = (i - self.a) * self.per if self.a else i * self.per
        return i

    def __exit__(self, *e):
        assert e[0] is not None or self.s.n - self.n0 == self.per, (self.s.n - self.n0, self.per)
        self.s.dyn = 0
        self.s.n = self.n0 + self.per * (self.b - self.a)
        return self.cm.__exit__(*e)


def build(nc, weights, vecs, consts, xT, x, mem, rows, gws, gbs, subkeys, w_down, w_up, out):
    ctx = ExitStack()
    with ctx:
        BASE = 16512
        SMALL = 15872
        UB = 8192
        at = [BASE]

        def small(name, shape, dt=F32):
            size = int(np.prod(shape[1:])) * 4
            t = nc.alloc_sbuf_tensor_at(name, shape, dt, offset=at[0])
            at[0] += (size + 31) // 32 * 32
            assert at[0] <= BASE + SMALL, (name, at[0] - BASE)
            return t

        def unit(name, u, shape, dt=F32, off=0):
            size = int(np.prod(shape[1:])) * 4
            o = BASE + SMALL + u * UB + off
            assert o + size <= BASE + SMALL + 24 * UB
            return nc.alloc_sbuf_tensor_at(name, shape, dt, offset=o)

        def sem(name):
            return ctx.enter_context(nc.semaphore(name))

        con = small("con", [P, NCON])
        vec = small("vec", [P, NVEC])

        def C(n):
            o, k = CON[n]
            return con[:, o:o + k]

        ident, ones = C("ident"), C("ones")
        raw = [unit(f"raw{s}", s, [P, DC, 256]) for s in range(4)]
        opA = unit("opA", 8, [P, DC, T])
        opB = unit("opB", 10, [P, DC, T])
        opC = unit("opC", 12, [P, DC, T])
        Q = unit("Q", 14, [P, HEADS, T])
        FK = unit("FK", 15, [P, HEADS, T])
        KE = unit("KE", 16, [P, HEADS, T])
        G = unit("G", 17, [P, HEADS, T])
        EG = unit("EG", 18, [P, HEADS, T])
        KI = unit("KI", 19, [P, HEADS, T])
        VN = unit("VN", 15, [P, MT, HEADS, P])
        KEe = unit("KEe", 17, [P, MT, HEADS, P])
        KEo = unit("KEo", 18, [P, MT, HEADS, P])
        PT = unit("PT", 20, [P, MT, HEADS, P])
        S = unit("S", 21, [P, 2, HEADS, P])
        OG = unit("OG", 22, [P, HEADS, T])
        PV = unit("PV", 23, [P, DC, T])
        sumA = unit("sumA", 12, [P, DC, T + 16])
        sumB = unit("sumB", 12, [P, 6, T + 16], off=8 * (T + 16) * 4)
        GA = unit("GA", 19, [P, DC, T])
        GB = unit("GB", 16, [P, DC, T])
        SQ = unit("SQ", 20, [P, HEADS, MT, P])
        DG = unit("DG", 17, [P, HEADS * MT, P])
        MB = unit("MB", 14, [P, DC, T])
        AM = unit("AM", 18, [P, 2, T])
        MEM = unit("MEM", 21, [P, MT, D])
        XR = unit("XR", 23, [P, MT, D])
        LNR = unit("LNR", 22, [P, 2, D])
        HT = unit("HT", 14, [P, FF // P, T])
        RL = unit("RL", 20, [P, 2, T])
        KX = unit("KX", 8, [P, XH, T])
        VX = unit("VX", 8, [P, MT, XH * XHD], off=4096)
        XN = unit("XN", 21, [P, MT, D])
        GA2 = unit("GA2", 14, [P, DC, T])
        GB2 = unit("GB2", 15, [P, DC, T])
        QR = unit("QR", 16, [P, 2, 2, T])
        KR = unit("KR", 16, [P, 2, 2, T], off=4096)
        V2 = unit("V2", 17, [P, MT, 512])
        GU = unit("GU", 17, [P, 4, T], off=4096)
        GV = unit("GV", 18, [P, MT, 512])
        WS = unit("WS", 18, [P, 8, P], off=4096)
        R1 = unit("R1", 9, [P, 2, T])
        R2 = unit("R2", 9, [P, 2, T], off=2048)
        AS = unit("AS", 19, [P, 4, 384])
        ATT = unit("ATT", 20, [P, 4, 384])
        AT = unit("AT", 10, [P, 4, T])
        GM = unit("GM", 11, [P, 4, T])
        GR = unit("GR", 20, [P, 512], off=6144)
        BS = unit("BS", 19, [P, 4, P], off=6144)
        ZB = unit("ZB", 21, [P, 2, MT, P])
        MA = unit("MA", 9, [P, DC, T])
        QX = unit("QX", 16, [P, XH, T])
        XS = unit("XS", 19, [P, XH * MT, T])
        XT = unit("XT", 20, [P, XH, 2, T])
        AXo = unit("AXo", 12, [P, 4, T])
        HN = unit("HN", 21, [P, MT, D])
        QP = unit("QP", 14, [P, 16, T])
        SK = unit("SK", 16, [P, 16, NK])
        SC = unit("SC", 17, [P, MT, 16, NK])
        RD = [unit(f"RD{s}", s // 2, [P, D], off=4096 * (s % 2)) for s in range(8)]
        RU = [unit(f"RU{s}", 4 + s // 2, [P, D], off=4096 * (s % 2)) for s in range(8)]
        DIAG = unit("DIAG", 19, [P, TOPK, P])
        JUNK = unit("JUNK", 20, [P, D])
        YO = unit("YO", 8, [P, MT, D])

        lbd = small("lbd", [P, 16])
        lb = small("lb", [P, 8])
        lbx = small("lbx", [P, 8])
        DEC = small("DEC", [P, NCH, HEADS])
        st16 = small("st16", [P, 16])
        bst = small("bst", [P, MT, 4, 6])
        mv = small("mv", [P, MT, 2])
        rst = small("rst", [P, MT])
        ssq = small("ssq", [P, MT, 4])
        msq = small("msq", [P, MT])
        mrs = small("mrs", [P, MT])
        amx = small("amx", [P, 8])
        asm = small("asm", [P, 8])
        IDX = small("IDX", [P, 16, TOPK], U32)
        cur = small("cur", [P, 3, TOPK], U32)
        GW = small("GW", [P, 16, TOPK])
        dots = small("dots", [P, 2, TOPK])
        act_d = small("act_d", [P, 2, TOPK])
        coef = small("coef", [P, 2, TOPK])
        sS = small("sS", [P, 2, NK])
        sW = small("sW", [P, 256])
        cand = small("cand", [P, 16, 16])
        eq = small("eq", [P, 16, 16])
        tv = small("tv", [P, 2, 16])
        ti = small("ti", [P, 2, 16], U32)
        tif = small("tif", [P, 2, 16])
        cv = small("cv", [P, 16])
        cp = small("cp", [P, 2, 16], U32)
        cpf = small("cpf", [P, 2, 16])
        ef = small("ef", [P, 2, 16])
        gx = small("gx", [P, 16])
        gs = small("gs", [P, 2])

        psum = ctx.enter_context(nc.psum_tensor("ps", [P, 8, 512], F32))

        def bank(r):
            return psum[:, r % 2, :]

        def aux(a):
            return psum[:, 2 + a % 2, :]

        raw_ready = [sem(f"raw_ready{s}") for s in range(4)]
        gemm_done = sem("gemm_done")
        drained = [sem(f"drained{s}") for s in range(2)]
        aux_done = sem("aux_done")
        aux_drained = [sem(f"aux_drained{s}") for s in range(2)]
        small_in, x_in, xr_in, mem_in = sem("small_in"), sem("x_in"), sem("xr_in"), sem("mem_in")
        rows_in, gml_in, sk_in, rows2_in, rows3_in = (
            sem("rows_in"), sem("gml_in"), sem("sk_in"), sem("rows2_in"), sem("rows3_in"))
        dve_step, act_step, pool_step = sem("dve_step"), sem("act_step"), sem("pool_step")
        lb_diff, lb_exp = sem("lb_diff"), sem("lb_exp")
        f_ready, logf_ready, g_ready = sem("f_ready"), sem("logf_ready"), sem("g_ready")
        eg_ready, ki_exp, kd_ready, ke_exp = sem("eg_ready"), sem("ki_exp"), sem("kd_ready"), sem("ke_exp")
        hg_ready, odd_done = sem("hg_ready"), sem("odd_done")
        intra_done, o_done, sq_done, o_var, o_std = (
            sem("intra_done"), sem("o_done"), sem("sq_done"), sem("o_var"), sem("o_std"))
        diag_ready, o_ready, pooled_ready, m_ready = (
            sem("diag_ready"), sem("o_ready"), sem("pooled_ready"), sem("m_ready"))
        xr_free, mem_free = sem("xr_free"), sem("mem_free")
        mem_sq, mem_ms, mem_sd, mem_z = sem("mem_sq"), sem("mem_ms"), sem("mem_sd"), sem("mem_z")
        ln_var, ln_std, ln_z, ln_op = sem("ln_var"), sem("ln_std"), sem("ln_z"), sem("ln_op")
        relu_done, h_ready, x_res = sem("relu_done"), sem("h_ready"), sem("x_res")
        rms_sq, rms_ms, rms_sd, rms_z, rms_op = (
            sem("rms_sq"), sem("rms_ms"), sem("rms_sd"), sem("rms_z"), sem("rms_op"))
        x_new = sem("x_new")
        quad_done, quad_read = sem("quad_done"), sem("quad_read")
        att_max, att_exp, att_p, att_t, att_op = (
            sem("att_max"), sem("att_exp"), sem("att_p"), sem("att_t"), sem("att_op"))
        gv_sq, gv_ms, gv_sd, gv_n, ws_masked, gm_op = (
            sem("gv_sq"), sem("gv_ms"), sem("gv_sd"), sem("gv_n"), sem("ws_masked"), sem("gm_op"))
        m2_ready, ax_op, hn_ready = sem("m2_ready"), sem("ax_op"), sem("hn_ready")
        top_v, top_e, idx_ready = sem("top_v"), sem("top_e"), sem("idx_ready")
        rd_in = [sem(f"rd_in{s}") for s in range(8)]
        ru_in = [sem(f"ru_in{s}") for s in range(8)]
        dot_done, gelu_done, coef_ready, dg_ready, up_done = (
            sem("dot_done"), sem("gelu_done"), sem("coef_ready"), sem("dg_ready"), sem("up_done"))
        fin_x, fin_sq, fin_ms, fin_sd, fin_y, stored = (
            sem("fin_x"), sem("fin_sq"), sem("fin_ms"), sem("fin_sd"), sem("fin_y"), sem("stored"))

        def group(eng, stage, j):
            last = UNIT[stage] + (4 * j + 3 if stage == "down" else j)
            eng.wait_ge(gemm_done, last + 1)
            return bank(RING[stage] + j)

        def drain(ins, stage, j):
            ins.then_inc(drained[(RING[stage] + j) % 2], 1)

        def wait_drained(eng, stage, j):
            r = RING[stage] + j
            eng.wait_ge(drained[r % 2], r // 2 + 2)

        def wait_stage(eng, stage, n):
            for j in range(max(0, n - 2), n):
                wait_drained(eng, stage, j)

        def batch(eng, name, j=0):
            a = AUX[name] + j
            eng.wait_ge(aux_done, a + 1)
            return aux(a)

        def drain_aux(ins, name, j=0):
            ins.then_inc(aux_drained[(AUX[name] + j) % 2], 1)

        def wait_aux(eng, name, j=0):
            a = AUX[name] + j
            eng.wait_ge(aux_drained[a % 2], a // 2 + 1)

        def v3(ap, n):
            return ap.rearrange("p (a b) -> p a b", a=n)

        block = ctx.enter_context(nc.Block())

        @block.sync
        def _(sp):
            sp.dma_start(con[:, :], consts).then_inc(small_in, 16)
            sp.dma_start(vec[:, :], vecs).then_inc(small_in, 16)
            sp.dma_start(opA[:, :, :], xT).then_inc(x_in, 16)

            def load(b, s, used):
                if used is not None:
                    sp.wait_ge(gemm_done, used)
                sp.dma_start(raw[s][:, :, :].rearrange("p a b -> p (a b)"),
                             weights[b] if isinstance(b, int) else
                             weights[bass.ds(b, 1)].rearrange("a p n -> (a p) n")
                             ).then_inc(raw_ready[s], 16)

            b = 0
            while b < NBLOCKS:
                n = 0
                if b % 4 == 0 and b >= 4:
                    d = last_unit[b - 4] - b
                    while b + n < NBLOCKS and last_unit[b + n - 4] - (b + n) == d:
                        n += 1
                    n = n // 4 * 4
                if n >= 8:
                    with sp.Fori(0, n // 4) as i:
                        for s in range(4):
                            load(i * 4 + (b + s), s, i * 4 + (b + s + d + 1))
                    b += n
                else:
                    load(b, b % 4, last_unit[b - 4] + 1 if b >= 4 else None)
                    b += 1
            sp.wait_ge(fin_y, 2)
            sp.dma_start(out.rearrange("(m p) d -> p m d", p=P), YO[:, :, :]).then_inc(stored, 16)
            sp.wait_ge(stored, 16)

        @block.tensor
        def _(pe):
            def take(b, n=1):
                for x_ in range(b, b + n):
                    pe.wait_ge(raw_ready[x_ % 4], 16 * (x_ // 4 + 1))

            def free_bank(r):
                pe.wait_ge(drained[r % 2], r // 2 + 1)

            def across(dst, w, op, k, first=True, last=True):
                for c in range(2):
                    for i in range(k):
                        mm = pe.matmul(dst[:, c * T:(c + 1) * T], w[:, i, c * P:(c + 1) * P],
                                       op[:, i, :], start=(i == 0), stop=(i == k - 1))
                return mm

            def down(dst, w, op, k, first=True, last=True):
                for m in range(MT):
                    for i in range(k):
                        mm = pe.matmul(dst[:, m * 256:(m + 1) * 256], op[:, i, m * P:(m + 1) * P],
                                       w[:, i, :], start=(first and i == 0 and m == 0),
                                       stop=(last and i == k - 1), skip_group_check=True)
                return mm

            def one(stage, j, op, kind):
                r, b = RING[stage] + j, BLOCK[stage] + j
                take(b)
                free_bank(r)
                kind(bank(r), raw[b % 4][:, :, :], op, DC).then_inc(gemm_done, 1)

            def halves(stage, j, op, kind):
                b = BLOCK[stage] + j
                take(b)
                for h in range(2):
                    r = RING[stage] + 2 * j + h
                    free_bank(r)
                    kind(bank(r), raw[b % 4][:, 4 * h:4 * h + 4, :], op, 4).then_inc(gemm_done, 1)

            def free_aux(name, j=0):
                a = AUX[name] + j
                if a >= 2:
                    pe.wait_ge(aux_drained[a % 2], a // 2)
                return aux(a)

            def transposes(name, j, pieces):
                dst = free_aux(name, j)
                for n, src in enumerate(pieces):
                    mm = pe.transpose(dst[:, n * P:(n + 1) * P], src, ident)
                mm.then_inc(aux_done, 1)

            def to_across(name, src, j):
                transposes(name, j, [src[:, m, c * P:(c + 1) * P] for c in (2 * j, 2 * j + 1)
                                     for m in range(MT)])

            pe.wait_ge(small_in, 32)
            pe.wait_ge(x_in, 16)
            with pe.Fori(0, 2) as i:
                for s in range(4):
                    pe.wait_ge(raw_ready[s], i * 16 + 16)
                    pe.wait_ge(drained[s % 2], i * 2 + (s // 2 + 1))
                    across(bank(s), raw[s][:, :, :], opA, DC).then_inc(gemm_done, 1)
            for j in range(4):
                one("i", j, opA, down)

            def ke_turn(n):
                m, q = n // 2, n % 2
                if n == 0:
                    pe.wait_ge(hg_ready, 3)
                transposes("kT", n, [KE[:, 4 * q + h, m * P:(m + 1) * P] for h in range(4)])

            def scores(n):
                m, q = n // 2, n % 2
                dst = free_aux("sc", n)
                for h in range(4):
                    t = slice(m * P, (m + 1) * P)
                    mm = pe.matmul(dst[:, h * P:(h + 1) * P], KI[:, 4 * q + h, t], Q[:, 4 * q + h, t],
                                   start=True, stop=True)
                mm.then_inc(aux_done, 1)

            def intra(q):
                wait_aux(pe, "sc", 2)
                wait_aux(pe, "sc", 3)
                for h in range(4 * q, 4 * q + 4):
                    dst = psum[:, 4 + h // 2, (h % 2) * T:(h % 2 + 1) * T]
                    for m in range(MT):
                        mm = pe.matmul(dst[:, m * P:(m + 1) * P], VN[:, m, h, :], PT[:, m, h, :],
                                       start=(h % 2 == 0 and m == 0), stop=True,
                                       skip_group_check=True)
                mm.then_inc(intra_done, 1)

            def chunk(c):
                m, g, ke = c // 8, (c % 8) // 2, (KEe, KEo)[c % 2]
                rows_ = slice(32 * g, 32 * g + 32)
                if c < NCH - 1:
                    for half in range(2):
                        dst = free_aux("U", 2 * c + half)
                        for h in range(4):
                            mm = pe.matmul(dst[:, h * P:(h + 1) * P], ke[rows_, m, 4 * half + h, :],
                                           VN[rows_, m, 4 * half + h, :], start=True, stop=True)
                        mm.then_inc(aux_done, 1)
                if c > 0:
                    wait_aux(pe, "U", 2 * c - 2)
                    wait_aux(pe, "U", 2 * c - 1)
                    for h in range(HEADS):
                        t0 = (h % 2) * T + c * CH
                        mm = pe.matmul(psum[:, 4 + h // 2, t0:t0 + CH], S[:, c % 2, h, :],
                                       Q[:, h, c * CH:(c + 1) * CH], start=False, stop=True,
                                       skip_group_check=True)
                    if c == NCH - 1:
                        mm.then_inc(o_done, 1)

            one("pv", 0, opA, across)
            ke_turn(0)
            ke_turn(1)
            one("pv", 1, opA, across)
            ke_turn(2)
            ke_turn(3)
            one("pv", 2, opA, across)
            scores(0)
            scores(1)
            one("pv", 3, opA, across)
            scores(2)
            scores(3)
            one("og", 0, opA, across)
            intra(0)
            one("og", 1, opA, across)
            intra(1)
            for n in range(8):
                st, j = [("og", 2), ("og", 3), ("ga", 0), ("ga", 1), ("ga", 2), ("ga", 3), ("gb", 0),
                         ("gb", 1)][n]
                one(st, j, opA, across)
                chunk(2 * n)
                chunk(2 * n + 1)
            one("gb", 2, opA, across)
            one("gb", 3, opA, across)

            pe.wait_ge(sq_done, 1)
            dst = free_aux("osum")
            for n in range(HEADS * MT):
                mm = pe.matmul(dst[:, n:n + 1], SQ[:, n // MT, n % MT, :], ones[:, 0:1],
                               start=True, stop=True)
            mm.then_inc(aux_done, 1)
            pe.wait_ge(pooled_ready, 1)

            def pool_group(g):
                r = RING["pool"] + g
                free_bank(r)
                across(bank(r), raw[BLOCK["pool"] % 4][:, 2 * g:2 * g + 2, :],
                       opB[:, 2 * g:2 * g + 2, :], 2).then_inc(gemm_done, 1)

            take(BLOCK["pool"])
            pool_group(0)
            pool_group(1)
            for j in range(4):
                if j == 0:
                    pe.wait_ge(diag_ready, 1)
                dst = free_aux("obc", j)
                pe.matmul(dst, ones, DG[:, 4 * j:4 * j + 4, :].rearrange("p a b -> p (a b)"),
                          start=True, stop=True).then_inc(aux_done, 1)
            pool_group(2)
            pool_group(3)
            pe.wait_ge(o_ready, 4)
            for j in range(4):
                one("wa", j, opC, across)
            pe.wait_ge(mem_z, 1)
            for j in range(4):
                to_across("memT", MEM, j)
            pe.wait_ge(m_ready, 4)
            for j in range(4):
                one("wo", j, opA, down)
            wait_aux(pe, "memT", 2)
            wait_aux(pe, "memT", 3)
            for j in range(2):
                one("xk", j, opB, across)
            pe.wait_ge(ln_z, 1)
            for j in range(4):
                to_across("ln1T", XR, j)
            wait_aux(pe, "ln1T", 2)
            wait_aux(pe, "ln1T", 3)
            b0, r0 = BLOCK["up"], RING["up"]
            with pe.Fori(0, 4) as i:
                for s in range(4):
                    b, r = b0 + s, r0 + s
                    pe.wait_ge(raw_ready[b % 4], i * 16 + 16 * (b // 4 + 1))
                    pe.wait_ge(drained[r % 2], i * 2 + (r // 2 + 1))
                    across(bank(r), raw[b % 4][:, :, :], opC, DC).then_inc(gemm_done, 1)
            for j in range(4):
                r = RING["down"] + j
                free_bank(r)
                for k in range(4):
                    b = BLOCK["down"] + 4 * j + k
                    take(b)
                    if j == 0:
                        pe.wait_ge(h_ready, 4 * k + 4)
                    down(bank(r), raw[b % 4][:, :, :], HT[:, 8 * k:8 * k + 8, :], DC,
                         first=(k == 0), last=(k == 3)).then_inc(gemm_done, 1)
            for j in range(2):
                one("xv", j, opB, down)
            pe.wait_ge(rms_z, 1)
            for j in range(4):
                to_across("h2T", XN, j)
            wait_aux(pe, "h2T", 2)
            wait_aux(pe, "h2T", 3)
            for st in ("q2", "k2"):
                for j in range(2):
                    one(st, j, opC, across)
            for j in range(2):
                one("v2", j, opC, down)

            def att_scores(a):
                if a == 0:
                    wait_stage(pe, "k2", 2)
                else:
                    pe.wait_ge(quad_read, 2)
                for part in range(2):
                    for h in range(4):
                        rw = slice(32 * h, 32 * h + 32)
                        dst = psum[:, 4 + h, :]
                        mm = pe.matmul(dst[:, 0:P], QR[rw, a, part, 0:P], KR[rw, a, part, 0:P],
                                       start=(part == 0), stop=(part == 1), skip_group_check=True)
                        mm = pe.matmul(dst[:, P:3 * P], QR[rw, a, part, P:T], KR[rw, a, part, :],
                                       start=False, stop=(part == 1), skip_group_check=True)
                mm.then_inc(quad_done, 1)

            def att_turn(a):
                pe.wait_ge(att_p, a + 1)
                for h in range(4):
                    for n in range(3):
                        mm = pe.transpose(psum[:, 4 + h, n * P:(n + 1) * P],
                                          AS[:, h, n * P:(n + 1) * P], ident)
                mm.then_inc(quad_done, 1)

            def att_values(a):
                pe.wait_ge(att_t, a + 1)
                if a == 0:
                    wait_stage(pe, "v2", 2)
                dst = free_aux(f"pv{a}")
                for h in range(4):
                    head = 4 * a + h
                    o = dst[64 * (head % 2):64 * (head % 2) + 64, (h // 2) * T:(h // 2 + 1) * T]
                    vs = slice(head * MHD, (head + 1) * MHD)
                    pe.matmul(o, V2[:, 0, vs], ATT[:, h, 0:T], start=True, stop=False,
                              skip_group_check=True)
                    mm = pe.matmul(o[:, P:T], V2[:, 1, vs], ATT[:, h, T:3 * P], start=False,
                                   stop=True, skip_group_check=True)
                mm.then_inc(aux_done, 1)

            def spatial(n):
                dst = free_aux("z", n)
                for c in range(2):
                    for m in range(MT):
                        for half in range(2):
                            g = 2 * (2 * n + c) + half
                            mm = pe.matmul(dst[64 * half:64 * half + 64,
                                               (c * MT + m) * P:(c * MT + m + 1) * P],
                                           GV[:, m, g * 64:(g + 1) * 64], WS[:, g, :],
                                           start=True, stop=True, skip_group_check=True)
                mm.then_inc(aux_done, 1)

            att_scores(0)
            for j in range(2):
                one("gu", j, opC, across)
            for j in range(2):
                one("gv", j, opC, down)
            att_turn(0)
            one("ga2", 0, opC, across)
            att_scores(1)
            one("ga2", 1, opC, across)
            att_values(0)
            one("ga2", 2, opC, across)
            one("ga2", 3, opC, across)
            att_turn(1)
            pe.wait_ge(gv_n, 2)
            pe.wait_ge(ws_masked, 1)
            one("gb2", 0, opC, across)
            att_values(1)
            one("gb2", 1, opC, across)
            spatial(0)
            spatial(1)
            one("gb2", 2, opC, across)
            one("gb2", 3, opC, across)
            pe.wait_ge(att_op, 2)
            for j in range(2):
                halves("ma", j, AT, across)
            pe.wait_ge(gm_op, 2)
            for j in range(2):
                halves("gm", j, GM, across)
            pe.wait_ge(m2_ready, 4)
            for j in range(4):
                one("wo2", j, opC, down)
            pe.wait_ge(rms_z, 2)
            for j in range(4):
                to_across("h3T", XN, j)
            wait_aux(pe, "h3T", 2)
            wait_aux(pe, "h3T", 3)
            for j in range(2):
                one("xq", j, opB, across)
            wait_stage(pe, "xq", 2)
            wait_stage(pe, "xk", 2)
            for h in range(XH):
                for m in range(MT):
                    mm = pe.matmul(psum[:, 4 + h, m * T:(m + 1) * T], QX[:, h, m * P:(m + 1) * P],
                                   KX[:, h, :], start=True, stop=True)
            mm.then_inc(quad_done, 1)
            pe.wait_ge(att_p, 3)
            for h in range(XH):
                for s in range(2):
                    for m in range(MT):
                        mm = pe.transpose(psum[:, 4 + h, (s * MT + m) * P:(s * MT + m + 1) * P],
                                          XS[:, h * MT + m, s * P:(s + 1) * P], ident)
            mm.then_inc(quad_done, 1)
            pe.wait_ge(att_t, 3)
            wait_stage(pe, "xv", 2)
            for n in range(2):
                dst = free_aux("xpv", n)
                for hh in range(2):
                    h = 2 * n + hh
                    for s in range(2):
                        mm = pe.matmul(dst[:, hh * T:(hh + 1) * T], VX[:, s, h * P:(h + 1) * P],
                                       XT[:, h, s, :], start=(s == 0), stop=(s == 1))
                mm.then_inc(aux_done, 1)
            pe.wait_ge(ax_op, 2)
            for j in range(2):
                halves("xo", j, AXo, down)
            pe.wait_ge(hn_ready, 2)
            for j in range(4):
                to_across("h4T", HN, j)
            wait_aux(pe, "h4T", 2)
            wait_aux(pe, "h4T", 3)
            b0, r0 = BLOCK["pq"], RING["pq"]
            with pe.Fori(0, 2) as i:
                for s in range(4):
                    b, r = b0 + s, r0 + s
                    pe.wait_ge(raw_ready[b % 4], i * 16 + 16 * (b // 4 + 1))
                    pe.wait_ge(drained[r % 2], i * 2 + (r // 2 + 1))
                    across(bank(r), raw[b % 4][:, :, :], opB, DC).then_inc(gemm_done, 1)
            wait_stage(pe, "pq", 8)
            pe.wait_ge(sk_in, 16)
            for n in range(8):
                m, q = n // 4, n % 4
                dst = free_aux("psc", n)
                for k in range(4):
                    mm = pe.matmul(dst[:, k * P:(k + 1) * P], QP[:, 4 * q + k, m * P:(m + 1) * P],
                                   SK[:, 4 * q + k, :], start=True, stop=True)
                mm.then_inc(aux_done, 1)
            for m in range(MT):
                for n in range(2):
                    pe.matmul(psum[:, 4 + 2 * m + n, :], C("zero").broadcast_to([P, P]),
                              SK[:, 0:4, :].rearrange("p a b -> p (a b)"), start=True, stop=False,
                              skip_group_check=True)
                with pe.Fori(0, 8) as h:
                    for k in range(TOPK):
                        it = h + 8 * m
                        if k % 8 == 0:
                            pe.wait_ge(dg_ready, it * 2 + (k // 8 + 1))
                        pe.wait_ge(ru_in[k % 8], it * 32 + 16 * (k // 8 + 1))
                        for n in range(2):
                            mm = pe.matmul(psum[:, 4 + 2 * m + n, :], DIAG[:, k, :],
                                           RU[k % 8][:, n * 512:(n + 1) * 512], start=False,
                                           stop=True, skip_group_check=True)
                        mm.then_inc(up_done, 1)

        @block.scalar
        def _(act):
            st = Steps(act, act_step)
            act.wait_ge(small_in, 32)
            act.wait_ge(lb_diff, 1)
            act.activation(lbd[:, :], lbd[:, :], ACT.Exp).then_inc(lb_exp, 1)
            for j in range(4):
                pb = group(act, "f", j)
                drain(act.activation(FK[:, 2 * j:2 * j + 2, :], v3(pb, 2), ACT.Sigmoid), "f", j)
            for j in range(4):
                pb = group(act, "q", j)
                drain(act.activation(Q[:, 2 * j:2 * j + 2, :], v3(pb, 2), ACT.Silu), "q", j)
            act.wait_ge(f_ready, 1)
            act.activation(KE[:, :, :], FK[:, :, :], ACT.Ln).then_inc(logf_ready, 1)
            act.wait_ge(g_ready, 1)
            act.activation(EG[:, :, :], G[:, :, :], ACT.Exp).then_inc(eg_ready, 1)
            act.activation(KI[:, :, :], G[:, :, :], ACT.Exp, scale=-1.0).then_inc(ki_exp, 1)
            act.wait_ge(kd_ready, 1)
            act.activation(KE[:, :, :], KE[:, :, :], ACT.Exp).then_inc(ke_exp, 1)
            for j in range(4):
                pb = group(act, "pv", j)
                drain(act.activation(PV[:, 2 * j:2 * j + 2, :], v3(pb, 2), ACT.Copy), "pv", j)
                for n in (2 * j, 2 * j + 1) if j < 2 else ():
                    pa = batch(act, "kT", n)
                    act.wait_ge(hg_ready, 3)
                    act.activation(KEo[:, n // 2, 4 * (n % 2):4 * (n % 2) + 4, :], v3(pa, 4), ACT.Copy,
                                   scale=C("odd")).then_inc(odd_done, 1)
            for st_, dst in (("og", OG), ("ga", GA), ("gb", GB)):
                if st_ == "ga":
                    wait_aux(act, "sc", 2)
                    wait_aux(act, "sc", 3)
                for j in range(4):
                    pb = group(act, st_, j)
                    drain(act.activation(dst[:, 2 * j:2 * j + 2, :], v3(pb, 2), ACT.Sigmoid), st_, j)
            act.wait_ge(pooled_ready, 1)
            act.dma_start(XR[:, :, :], x.rearrange("(m p) d -> p m d", p=P)).then_inc(xr_in, 16)
            act.wait_ge(o_done, 1)
            act.activation(SQ[:, :, :, :].rearrange("p h m t -> p (h m t)"),
                           psum[:, 4:8, :].rearrange("p a b -> p (a b)"), ACT.Square
                           ).then_inc(sq_done, 1)
            act.dma_start(MEM[:, :, :], mem.rearrange("(m p) d -> p m d", p=P)).then_inc(mem_in, 16)
            act.wait_ge(o_var, 1)
            act.activation(st16[:, :], st16[:, :], ACT.Sqrt).then_inc(o_std, 1)
            act.wait_ge(mem_in, 16)
            act.wait_ge(diag_ready, 1)
            for m in range(MT):
                st.do(act.activation(SQ[:, 4 * m:4 * m + 4, :, :].rearrange("p a b c -> p (a b c)"),
                                     MEM[:, m, :], ACT.Square, accum_out=msq[:, m:m + 1]))
            st.sync()
            act.activation(mrs[:, :], msq[:, :], ACT.Copy).then_inc(mem_sq, 1)
            act.wait_ge(mem_ms, 1)
            act.activation(mrs[:, :], mrs[:, :], ACT.Sqrt).then_inc(mem_sd, 1)
            wait_stage(act, "gb", 4)
            act.wait_ge(o_ready, 4)
            act.dma_start(LNR[:, :, :], rows[0:2, :].partition_broadcast(P)).then_inc(rows_in, 16)
            for j in range(4):
                pa = batch(act, "memT", j)
                for c in range(2):
                    ins = act.activation(opB[:, 2 * j + c, :], pa[:, c * T:(c + 1) * T], ACT.Copy,
                                         scale=vec[:, VEC["memg"] + 2 * j + c:VEC["memg"] + 2 * j + c + 1])
                    if c == 0:
                        st.do(ins)
                drain_aux(ins, "memT", j)
            act.wait_ge(ln_var, 1)
            act.activation(rst[:, :], rst[:, :], ACT.Sqrt).then_inc(ln_std, 1)
            act.wait_ge(gemm_done, UNIT["wo"] + 4)
            for j in range(2):
                pb = group(act, "xk", j)
                drain(act.activation(KX[:, 2 * j:2 * j + 2, :], v3(pb, 2), ACT.Copy), "xk", j)
            r0 = RING["up"]
            with act.Fori(0, 4) as i:
                for s in range(4):
                    act.wait_ge(gemm_done, i * 4 + (UNIT["up"] + s + 1))
                    act.activation(RL[:, :, :], v3(bank(r0 + s), 2), ACT.Relu
                                   ).then_inc(drained[(r0 + s) % 2], 1)
                    act.wait_ge(drained[(r0 + s) % 2], i * 2 + ((r0 + s) // 2 + 2))
                    act.activation(HT[:, bass.ds(i * 8 + 2 * s, 2), :], RL[:, :, :], ACT.Square
                                   ).then_inc(h_ready, 1)
                    act.wait_ge(h_ready, i * 4 + (s + 1))
            act.wait_ge(x_res, 1)
            act.dma_start(LNR[:, :, :], rows[2:4, :].partition_broadcast(P)).then_inc(rows_in, 16)
            act.wait_ge(ln_var, 2)
            act.activation(rst[:, :], rst[:, :], ACT.Sqrt).then_inc(ln_std, 1)

            def mean_squares(n, dst, deps):
                for m in range(MT):
                    st.do(act.activation(dst[:, m, :], XR[:, m, :], ACT.Square,
                                         accum_out=ssq[:, m, 0:1]))
                st.sync()
                act.activation(rst[:, :], ssq[:, :, 0], ACT.Copy).then_inc(rms_sq, 1)
                act.wait_ge(rms_ms, n)
                act.activation(rst[:, :], rst[:, :], ACT.Sqrt).then_inc(rms_sd, 1)

            act.wait_ge(x_new, 1)
            mean_squares(1, XN, None)
            act.wait_ge(gemm_done, UNIT["down"] + 16)
            act.dma_start(GR[:, :], rows[4:5, 0:512].rearrange("a n -> (a n)").partition_broadcast(P)
                          ).then_inc(gml_in, 16)
            act.dma_start(WS[:, :, :], gws).then_inc(gml_in, 16)
            act.dma_start(BS[0:64, :, :], gbs[0].partition_broadcast(64)).then_inc(gml_in, 16)
            act.dma_start(BS[64:128, :, :], gbs[1].partition_broadcast(64)).then_inc(gml_in, 16)
            for j in range(2):
                pb = group(act, "xv", j)
                drain(act.activation(VX[:, :, 256 * j:256 * j + 256], v3(pb, 2), ACT.Copy), "xv", j)
            for j in range(2):
                pb = group(act, "v2", j)
                drain(act.activation(V2[:, :, 256 * j:256 * j + 256], v3(pb, 2), ACT.Copy), "v2", j)

            def exps(a):
                act.wait_ge(att_max, a + 1)
                for h in range(4):
                    for m in range(MT):
                        sl = slice(0, P) if m == 0 else slice(P, 3 * P)
                        ins = act.activation(AS[:, h, sl], AS[:, h, sl], ACT.Exp,
                                             bias=amx[:, 2 * h + m:2 * h + m + 1],
                                             accum_out=asm[:, 2 * h + m:2 * h + m + 1])
                        if (h, m) != (3, 1):
                            st.do(ins)
                ins.then_inc(att_exp, 1)

            def turned(a, n, src, dst):
                act.wait_ge(quad_done, n)
                act.activation(dst, src, ACT.Copy).then_inc(att_t, 1)

            exps(0)
            for j in range(2):
                pb = group(act, "gu", j)
                drain(act.activation(GU[:, 2 * j:2 * j + 2, :], v3(pb, 2), ACT.Gelu_apprx_tanh), "gu", j)
            for j in range(2):
                pb = group(act, "gv", j)
                drain(act.activation(GV[:, :, 256 * j:256 * j + 256], v3(pb, 2), ACT.Gelu_apprx_tanh),
                      "gv", j)
            turned(0, 2, psum[:, 4:8, 0:384], ATT[:, :, :])
            wait_stage(act, "gv", 2)
            act.wait_ge(rms_z, 1)
            for m in range(MT):
                st.do(act.activation(ZB[:, :, :, :].rearrange("p a b c -> p (a b c)"), GV[:, m, :],
                                     ACT.Square, accum_out=ssq[:, m, 1:2]))
                st.sync()
            act.activation(ssq[:, :, 2], ssq[:, :, 1], ACT.Copy).then_inc(gv_sq, 1)
            act.wait_ge(gv_ms, 1)
            act.activation(ssq[:, :, 2], ssq[:, :, 2], ACT.Sqrt).then_inc(gv_sd, 1)
            for j in range(4):
                pb = group(act, "ga2", j)
                drain(act.activation(GA2[:, 2 * j:2 * j + 2, :], v3(pb, 2), ACT.Sigmoid), "ga2", j)
            exps(1)
            act.wait_ge(aux_done, AUX["pv0"] + 1)
            turned(1, 4, psum[:, 4:8, 0:384], ATT[:, :, :])
            for j in range(4):
                pb = group(act, "gb2", j)
                drain(act.activation(GB2[:, 2 * j:2 * j + 2, :], v3(pb, 2), ACT.Sigmoid), "gb2", j)
            act.wait_ge(x_new, 2)
            mean_squares(2, XN, None)
            act.wait_ge(att_op, 2)
            for j in range(2):
                pb = group(act, "xq", j)
                drain(act.activation(QX[:, 2 * j:2 * j + 2, :], v3(pb, 2), ACT.Copy), "xq", j)
            act.wait_ge(att_max, 3)
            for n in range(8):
                h, m = n // 2, n % 2
                ins = act.activation(XS[:, n, :], psum[:, 4 + h, m * T:(m + 1) * T], ACT.Exp,
                                     bias=amx[:, n:n + 1], scale=float(XHD) ** -0.5,
                                     accum_out=asm[:, n:n + 1])
                if n < 7:
                    st.do(ins)
            ins.then_inc(att_exp, 1)
            turned(2, 6, psum[:, 4:8, :], XT[:, :, :, :].rearrange("p h s t -> p h (s t)"))
            act.dma_start(SK[:, :, :], subkeys).then_inc(sk_in, 16)
            act.wait_ge(x_new, 3)
            act.dma_start(LNR[:, :, :], rows[5:7, :].partition_broadcast(P)).then_inc(rows2_in, 16)
            mean_squares(3, HN, None)
            for j in range(8):
                pb = group(act, "pq", j)
                drain(act.activation(QP[:, 2 * j:2 * j + 2, :], v3(pb, 2), ACT.Copy), "pq", j)
            for n in range(8):
                pa = batch(act, "psc", n)
                drain_aux(act.activation(SC[:, n // 4, 4 * (n % 4):4 * (n % 4) + 4, :], v3(pa, 4),
                                         ACT.Copy), "psc", n)

            def gate_exp(it):
                act.wait_ge(top_v, it + 1)
                act.activation(gx[:, :], cv[:, :], ACT.Exp, bias=gs[:, 0:1],
                               accum_out=gs[:, 1:2]).then_inc(top_e, 1)

            def pass_(it, par):
                if not (isinstance(it, int) and it == 15):
                    gate_exp(it + 1)
                act.wait_ge(dot_done, it * 16 + 16)
                act.activation(act_d[:, par, :], dots[:, par, :], ACT.Gelu_apprx_tanh
                               ).then_inc(gelu_done, 1)
                act.wait_ge(coef_ready, it + 1)
                for k in range(TOPK):
                    if k % 8 == 0 and not (isinstance(it, int) and it == 0):
                        act.wait_ge(up_done, it * 16 + (k - 8))
                    ins = act.activation(DIAG[:, k, :], ident, ACT.Copy, scale=coef[:, par, k:k + 1])
                    if k % 8 == 7:
                        ins.then_inc(dg_ready, 1)

            gate_exp(0)
            pass_(0, 0)
            pass_(1, 1)
            with act.Fori(1, 7) as i:
                pass_(i * 2, 0)
                pass_(i * 2 + 1, 1)
            pass_(14, 0)
            pass_(15, 1)
            for m in range(MT):
                act.wait_ge(fin_x, m + 1)
                act.activation(YO[:, m, :], XR[:, m, :], ACT.Square, accum_out=ssq[:, m, 0:1]
                               ).then_inc(fin_sq, 1)
                act.wait_ge(fin_ms, m + 1)
                act.activation(rst[:, m:m + 1], rst[:, m:m + 1], ACT.Sqrt).then_inc(fin_sd, 1)

        @block.vector
        def _(dve):
            st = Steps(dve, dve_step)
            for s in range(2):
                dve.engine_nop().then_inc(drained[s], 1)
            dve.wait_ge(small_in, 32)
            V = lambda n, c: vec[:, VEC[n] + c:VEC[n] + c + 1]
            l0, l1 = vec[:, VEC["lb0"]:VEC["lb0"] + 8], vec[:, VEC["lb1"]:VEC["lb1"] + 8]
            st.then(dve.tensor_tensor(lbx[:, :], l0, l1, ALU.max))
            st.do(dve.tensor_tensor(lbd[:, 0:8], l0, lbx[:, :], ALU.subtract))
            dve.tensor_tensor(lbd[:, 8:16], l1, lbx[:, :], ALU.subtract).then_inc(lb_diff, 1)
            dve.wait_ge(lb_exp, 1)
            st.then(dve.tensor_tensor(lb[:, :], lbd[:, 0:8], lbd[:, 8:16], ALU.add))
            st.then(dve.reciprocal(lb[:, :], lb[:, :]))
            st.then(dve.tensor_tensor(lb[:, :], lb[:, :], lbd[:, 0:8], ALU.mult))
            st.then(dve.tensor_scalar(lbx[:, :], lb[:, :], -1.0, 1.0, ALU.mult, ALU.add))
            for j in range(4):
                wait_drained(dve, "f", j)
                for h in (2 * j, 2 * j + 1):
                    ins = dve.tensor_scalar(FK[:, h, :], FK[:, h, :], lbx[:, h:h + 1], lb[:, h:h + 1],
                                            ALU.mult, ALU.add)
                    if h < 7:
                        st.do(ins)
            ins.then_inc(f_ready, 1)
            dve.wait_ge(logf_ready, 1)
            for h in range(HEADS):
                ins = dve.tensor_tensor_scan(G[:, h, :], C("reset"), KE[:, h, :], 0.0, ALU.mult, ALU.add)
                if h < 7:
                    st.do(ins)
            ins.then_inc(g_ready, 1)
            st.then(dve.tensor_scalar(FK[:, :, :], FK[:, :, :], -1.0, 1.0, ALU.mult, ALU.add))
            dve.wait_ge(g_ready, 1)
            g4 = G[:, :, :].rearrange("p h (c s) -> p (h c) s", s=CH)
            ke4 = KE[:, :, :].rearrange("p h (c s) -> p (h c) s", s=CH)
            dve.tensor_tensor(ke4, g4[:, :, CH - 1:CH].broadcast_to([P, HEADS * NCH, CH]), g4,
                              ALU.subtract).then_inc(kd_ready, 1)
            dve.wait_ge(eg_ready, 1)
            st.do(dve.tensor_copy(DEC[:, :, :].rearrange("p c h -> p h c"),
                                  EG[:, :, :].rearrange("p h (c s) -> p h c s", s=CH)[:, :, :, CH - 1]))
            wait_stage(dve, "q", 4)
            dve.scalar_tensor_tensor(out=Q[:, :, :], in0=Q[:, :, :], scalar=float(P) ** -0.5,
                                     in1=EG[:, :, :], op0=ALU.mult, op1=ALU.mult).then_inc(hg_ready, 1)
            dve.wait_ge(ki_exp, 1)
            dve.tensor_tensor(KI[:, :, :], KI[:, :, :], FK[:, :, :], ALU.mult).then_inc(hg_ready, 1)
            dve.wait_ge(ke_exp, 1)
            dve.tensor_tensor(KE[:, :, :], KE[:, :, :], FK[:, :, :], ALU.mult).then_inc(hg_ready, 1)
            dve.wait_ge(hg_ready, 3)
            for j in range(4):
                pb = group(dve, "i", j)
                drain(dve.tensor_copy(VN[:, :, 2 * j:2 * j + 2, :].rearrange("p m h v -> p m (h v)"),
                                      v3(pb, 2)), "i", j)
            st.do(dve.memset(PT[:, :, :, :], 0.0))
            st.then(dve.memset(S[:, 0, :, :], 0.0))
            for j in range(4):
                pa = batch(dve, "kT", j)
                dve.wait_ge(odd_done, j + 1)
                drain_aux(dve.tensor_scalar(KEe[:, j // 2, 4 * (j % 2):4 * (j % 2) + 4, :], v3(pa, 4),
                                            C("even"), None, ALU.mult), "kT", j)
            cm = C("cmask").bitcast(U32)
            for j in range(4):
                pa = batch(dve, "sc", j)
                for h in range(4):
                    ins = dve.copy_predicated(PT[:, j // 2, 4 * (j % 2) + h, :], cm,
                                              pa[:, h * P:(h + 1) * P])
                    if h < 3:
                        st.do(ins)
                drain_aux(ins, "sc", j)
            wait_stage(dve, "pv", 4)
            o = 16
            st.do(dve.memset(sumA[:, :, 0:o], 0.0))
            st.do(dve.memset(sumB[:, :, 0:o], 0.0))
            st.do(dve.tensor_copy(sumA[:, :, o:o + 1], PV[:, :, 0:1]))
            st.then(dve.tensor_tensor(sumA[:, :, o + 1:], PV[:, :, 1:], PV[:, :, 0:T - 1], ALU.add))
            st.then(dve.tensor_tensor(sumB[:, :, o:], sumA[:, 2:8, o:], sumA[:, 2:8, o - 2:o + T - 2],
                                      ALU.add))
            st.then(dve.tensor_tensor(sumA[:, 4:8, o:], sumB[:, 2:6, o:], sumB[:, 2:6, o - 4:o + T - 4],
                                      ALU.add))
            st.then(dve.tensor_tensor(sumB[:, 4:6, o:], sumA[:, 6:8, o:], sumA[:, 6:8, o - 8:o + T - 8],
                                      ALU.add))
            for g in range(4):
                w = 2 << g
                src = [sumA[:, 0:2], sumB[:, 0:2], sumA[:, 4:6], sumB[:, 4:6]][g]
                invc = C("invc")[:, 16 * g:16 * g + 16]
                st.do(dve.scalar_tensor_tensor(out=opB[:, 2 * g:2 * g + 2, 16:], in0=src[:, :, o + 16:],
                                               scalar=1.0 / w, in1=PV[:, 2 * g:2 * g + 2, 16:],
                                               op0=ALU.mult, op1=ALU.subtract))
                for c in range(2):
                    st.do(dve.tensor_tensor(src[:, c, o:o + 16], src[:, c, o:o + 16], invc, ALU.mult))
                st.sync()
                ins = dve.tensor_tensor(opB[:, 2 * g:2 * g + 2, 0:16], src[:, :, o:o + 16],
                                        PV[:, 2 * g:2 * g + 2, 0:16], ALU.subtract)
                if g < 3:
                    st.do(ins)
            ins.then_inc(pooled_ready, 1)
            def state(c, par, last=False):
                for half in range(2):
                    a = AUX["U"] + half
                    dve.wait_ge(aux_done, c * 2 + (a + 1))
                    for h in range(4 * half, 4 * half + 4):
                        ins = dve.scalar_tensor_tensor(
                            out=S[:, 1 - par, h, :], in0=S[:, par, h, :],
                            scalar=DEC[:, c, h:h + 1] if isinstance(c, int) else
                            DEC[:, bass.ds(c, 1), h:h + 1].rearrange("p a b -> p (a b)"),
                            in1=aux(half)[:, (h % 4) * P:(h % 4 + 1) * P], op0=ALU.mult, op1=ALU.add)
                    ins.then_inc(aux_drained[a % 2], 1)
                for half in range(2):
                    a = AUX["U"] + half
                    dve.wait_ge(aux_drained[a % 2], c + (a // 2 + 1))

            with dve.Fori(0, 7) as i:
                state(i * 2, 0)
                state(i * 2 + 1, 1)
            state(14, 0)
            dve.wait_ge(sq_done, 1)
            wait_stage(dve, "og", 4)
            for h in range(HEADS):
                st.do(dve.scalar_tensor_tensor(out=OG[:, h, :], in0=psum[:, 4 + h // 2,
                                               (h % 2) * T:(h % 2 + 1) * T], scalar=V("hg", h),
                                               in1=OG[:, h, :], op0=ALU.mult, op1=ALU.mult))
            pa = batch(dve, "osum")
            dve.tensor_scalar(st16[:, :], pa[:, 0:16], 1.0 / P, RMS_EPS, ALU.mult, ALU.add
                              ).then_inc(o_var, 1)
            dve.wait_ge(o_std, 1)
            st.then(dve.reciprocal(st16[:, :], st16[:, :]))
            drain_aux(dve.tensor_tensor(DG[:, :, :], ident.rearrange("p (a b) -> p a b", a=1)
                                        .broadcast_to([P, 16, P]),
                                        st16[:, :].rearrange("p (a b) -> p a b", b=1)
                                        .broadcast_to([P, 16, P]), ALU.mult), "osum")
            wait_aux(dve, "osum")
            dve.tensor_copy(lbd[:, 0:1], st16[:, 0:1]).then_inc(diag_ready, 1)
            for j in range(4):
                pa = batch(dve, "obc", j)
                ins = dve.tensor_tensor(opC[:, 2 * j:2 * j + 2, :], OG[:, 2 * j:2 * j + 2, :],
                                        v3(pa, 2), ALU.mult)
                drain_aux(ins, "obc", j)
                wait_aux(dve, "obc", j)
                dve.tensor_copy(lbd[:, 1:2], lbd[:, 0:1]).then_inc(o_ready, 1)
            dve.wait_ge(mem_sq, 1)
            dve.tensor_scalar(mrs[:, :], mrs[:, :], 1.0 / D, RMS_EPS, ALU.mult, ALU.add
                              ).then_inc(mem_ms, 1)
            dve.wait_ge(mem_sd, 1)
            st.then(dve.reciprocal(mrs[:, :], mrs[:, :]))
            st.do(dve.tensor_scalar(MEM[:, 0, :], MEM[:, 0, :], mrs[:, 0:1], None, ALU.mult))
            dve.tensor_scalar(MEM[:, 1, :], MEM[:, 1, :], mrs[:, 1:2], None, ALU.mult
                              ).then_inc(mem_z, 1)
            wait_stage(dve, "gb", 4)
            for j in range(4):
                pb = group(dve, "pool", j)
                st.do(dve.scalar_tensor_tensor(out=MB[:, 2 * j, :], in0=pb[:, 0:T], scalar=V("ps", 2 * j),
                                               in1=GB[:, 2 * j, :], op0=ALU.mult, op1=ALU.mult))
                drain(dve.scalar_tensor_tensor(out=MB[:, 2 * j + 1, :], in0=pb[:, T:], scalar=V("ps", 2 * j + 1),
                                               in1=GB[:, 2 * j + 1, :], op0=ALU.mult, op1=ALU.mult),
                      "pool", j)
            wait_stage(dve, "pool", 4)
            for j in range(4):
                pb = group(dve, "wa", j)
                if j:
                    dve.wait_ge(m_ready, j)
                drain(dve.tensor_tensor(AM[:, :, :], v3(pb, 2), GA[:, 2 * j:2 * j + 2, :], ALU.mult),
                      "wa", j)
                wait_drained(dve, "wa", j)
                dve.tensor_tensor(opA[:, 2 * j:2 * j + 2, :], AM[:, :, :], MB[:, 2 * j:2 * j + 2, :],
                                  ALU.add).then_inc(m_ready, 1)

            def norm(stage, n):
                for j in range(4):
                    pb = group(dve, stage, j)
                    sl = slice(256 * j, 256 * j + 256)
                    drain(dve.scalar_tensor_tensor(out=XR[:, :, sl], in0=XR[:, :, sl], scalar=ALPHA,
                                                   in1=v3(pb, 2), op0=ALU.mult, op1=ALU.add), stage, j)
                    wait_drained(dve, stage, j)
                    for m in range(MT):
                        st.do(dve.bn_stats(bst[:, m, j, :], XR[:, m, sl]))
                st.sync()
                for m in range(MT):
                    st.do(dve.bn_aggr(mv[:, m, :], bst[:, m, :, :]))
                st.sync()
                dve.tensor_scalar(rst[:, :], mv[:, :, 1], LN_EPS, None, ALU.add).then_inc(ln_var, 1)
                dve.wait_ge(ln_std, n)
                st.then(dve.reciprocal(rst[:, :], rst[:, :]))
                for m in range(MT):
                    ins = dve.tensor_scalar(XR[:, m, :], XR[:, m, :], mv[:, m, 0:1], rst[:, m:m + 1],
                                            ALU.subtract, ALU.mult)
                    if m == 0:
                        st.do(ins)
                ins.then_inc(ln_z, 1)
                dve.wait_ge(ln_z, n)

            def gain_and_bias():
                for m in range(MT):
                    st.do(dve.tensor_tensor(XR[:, m, :], XR[:, m, :], LNR[:, 0, :], ALU.mult))
                st.sync()
                st.do(dve.tensor_tensor(XR[:, 0, :], XR[:, 0, :], LNR[:, 1, :], ALU.add))
                return dve.tensor_tensor(XR[:, 1, :], XR[:, 1, :], LNR[:, 1, :], ALU.add)

            dve.wait_ge(xr_in, 16)
            norm("wo", 1)
            for j in range(4):
                pa = batch(dve, "ln1T", j)
                for c in (2 * j, 2 * j + 1):
                    ins = dve.tensor_scalar(opC[:, c, :], pa[:, (c % 2) * T:(c % 2 + 1) * T],
                                            V("ln1g", c), V("ln1b", c), ALU.mult, ALU.add)
                    if c % 2 == 0:
                        st.do(ins)
                drain_aux(ins, "ln1T", j)
            dve.wait_ge(rows_in, 16)
            gain_and_bias().then_inc(x_res, 1)
            dve.wait_ge(x_res, 1)
            norm("down", 2)
            dve.wait_ge(rows_in, 32)
            gain_and_bias().then_inc(x_new, 1)

            def rms(n, dst):
                dve.wait_ge(rms_sq, n)
                dve.tensor_scalar(rst[:, :], rst[:, :], 1.0 / D, RMS_EPS, ALU.mult, ALU.add
                                  ).then_inc(rms_ms, 1)
                dve.wait_ge(rms_sd, n)
                st.then(dve.reciprocal(rst[:, :], rst[:, :]))

            def rms_across(n, name, gain, op):
                rms(n, XN)
                for m in range(MT):
                    ins = dve.tensor_scalar(XN[:, m, :], XR[:, m, :], rst[:, m:m + 1], None, ALU.mult)
                    if m == 0:
                        st.do(ins)
                ins.then_inc(rms_z, 1)
                for j in range(4):
                    pa = batch(dve, name, j)
                    for c in (2 * j, 2 * j + 1):
                        ins = dve.tensor_scalar(op[:, c, :], pa[:, (c % 2) * T:(c % 2 + 1) * T],
                                                V(gain, c), None, ALU.mult)
                        if c % 2 == 0:
                            st.do(ins)
                    drain_aux(ins, name, j)

            rms_across(1, "h2T", "mixg", opC)
            cos, sin = (C(n).rearrange("p (a t) -> p a t", a=1).broadcast_to([P, 2, T])
                        for n in ("cos", "sin"))
            for stage, dst in (("q2", QR), ("k2", KR)):
                for j in range(2):
                    pb = group(dve, stage, j)
                    st.do(dve.tensor_tensor(R1[:, :, :], v3(pb, 2), cos, ALU.mult))
                    st.then(dve.tensor_tensor(R2[:, :, :], v3(pb, 2), sin, ALU.mult))
                    st.do(dve.tensor_tensor(dst[:, j, 0, :], R1[:, 0, :], R2[:, 1, :], ALU.subtract))
                    drain(dve.tensor_tensor(dst[:, j, 1, :], R1[:, 1, :], R2[:, 0, :], ALU.add), stage, j)
                    wait_drained(dve, stage, j)

            def att_softmax(a):
                dve.wait_ge(quad_done, 2 * a + 1)
                st.then(dve.scalar_tensor_tensor(
                    out=AS[:, :, :], in0=psum[:, 4:8, 0:384], scalar=float(MHD) ** -0.5,
                    in1=C("amask").rearrange("p (a b) -> p a b", a=1).broadcast_to([P, 4, 384]),
                    op0=ALU.mult, op1=ALU.add))
                am = amx[:, :].rearrange("p (h m) -> p h m", m=2)
                st.do(dve.tensor_reduce(am[:, :, 0], AS[:, :, 0:P], AX, ALU.max))
                st.then(dve.tensor_reduce(am[:, :, 1], AS[:, :, P:3 * P], AX, ALU.max))
                dve.tensor_scalar(amx[:, :], amx[:, :], -1.0, None, ALU.mult).then_inc(att_max, 1)

            def att_weights(a):
                dve.wait_ge(att_exp, a + 1)
                st.then(dve.reciprocal(asm[:, :], asm[:, :]))
                sm = asm[:, :].rearrange("p (h m) -> p h m", m=2)
                st.do(dve.tensor_tensor(AS[:, :, 0:P], AS[:, :, 0:P],
                                        sm[:, :, 0:1].broadcast_to([P, 4, P]), ALU.mult))
                dve.tensor_tensor(AS[:, :, P:3 * P], AS[:, :, P:3 * P],
                                  sm[:, :, 1:2].broadcast_to([P, 4, 2 * P]), ALU.mult
                                  ).then_inc(att_p, 1)

            att_softmax(0)
            dve.engine_nop().then_inc(quad_read, 1)
            att_weights(0)
            dve.wait_ge(gv_sq, 1)
            dve.tensor_scalar(ssq[:, :, 2], ssq[:, :, 2], 1.0 / 512, RMS_EPS, ALU.mult, ALU.add
                              ).then_inc(gv_ms, 1)
            dve.wait_ge(gv_sd, 1)
            st.then(dve.reciprocal(ssq[:, :, 3], ssq[:, :, 2]))
            dve.wait_ge(gml_in, 64)
            for m in range(MT):
                dve.scalar_tensor_tensor(out=GV[:, m, :], in0=GV[:, m, :], scalar=ssq[:, m, 3:4],
                                         in1=GR[:, :], op0=ALU.mult, op1=ALU.mult).then_inc(gv_n, 1)
            dve.wait_ge(att_t, 1)
            dve.engine_nop().then_inc(quad_read, 1)
            att_softmax(1)
            att_weights(1)

            def att_out(a):
                pa = batch(dve, f"pv{a}")
                drain_aux(dve.tensor_copy(AT[:, 2 * a:2 * a + 2, :], v3(pa, 2)), f"pv{a}")
                wait_aux(dve, f"pv{a}")
                dve.engine_nop().then_inc(att_op, 1)

            att_out(0)
            att_out(1)
            for n in range(2):
                pa = batch(dve, "z", n)
                bs = BS[:, 2 * n:2 * n + 2, :]
                for m in range(MT):
                    ins = dve.tensor_tensor(
                        ZB[:, :, m, :], pa.rearrange("p (c m t) -> p c m t", c=2, m=MT)[:, :, m, :],
                        bs, ALU.add)
                    if m == 0:
                        st.do(ins)
                drain_aux(ins, "z", n)
                wait_aux(dve, "z", n)
                dve.tensor_tensor(GM[:, 2 * n:2 * n + 2, :], ZB[:, :, :, :].rearrange("p c m t -> p c (m t)"),
                                  GU[:, 2 * n:2 * n + 2, :], ALU.mult).then_inc(gm_op, 1)
                dve.wait_ge(gm_op, n + 1)
            wait_stage(dve, "gb2", 4)
            for j in range(4):
                pb = group(dve, "ma", j)
                drain(dve.tensor_tensor(MA[:, 2 * j:2 * j + 2, :], v3(pb, 2),
                                        GA2[:, 2 * j:2 * j + 2, :], ALU.mult), "ma", j)
            wait_stage(dve, "ma", 4)
            for j in range(4):
                pb = group(dve, "gm", j)
                drain(dve.tensor_tensor(AM[:, :, :], v3(pb, 2), GB2[:, 2 * j:2 * j + 2, :], ALU.mult),
                      "gm", j)
                wait_drained(dve, "gm", j)
                dve.tensor_tensor(opC[:, 2 * j:2 * j + 2, :], AM[:, :, :], MA[:, 2 * j:2 * j + 2, :],
                                  ALU.add).then_inc(m2_ready, 1)
                dve.wait_ge(m2_ready, j + 1)

            def residual(stage):
                for j in range(4):
                    pb = group(dve, stage, j)
                    sl = slice(256 * j, 256 * j + 256)
                    drain(dve.tensor_tensor(XR[:, :, sl], XR[:, :, sl], v3(pb, 2), ALU.add), stage, j)
                wait_stage(dve, stage, 4)
                dve.engine_nop().then_inc(x_new, 1)

            residual("wo2")
            rms_across(2, "h3T", "xag", opB)
            dve.wait_ge(quad_done, 5)
            st.then(dve.tensor_reduce(amx[:, :].rearrange("p (h m) -> p h m", m=2),
                                      psum[:, 4:8, :].rearrange("p h (m t) -> p h m t", m=2),
                                      AX, ALU.max))
            dve.tensor_scalar(amx[:, :], amx[:, :], -float(XHD) ** -0.5, None, ALU.mult
                              ).then_inc(att_max, 1)
            dve.wait_ge(att_exp, 3)
            st.then(dve.reciprocal(asm[:, :], asm[:, :]))
            dve.tensor_tensor(XS[:, :, :], XS[:, :, :], asm[:, :].rearrange("p (a b) -> p a b", b=1)
                              .broadcast_to([P, 8, T]), ALU.mult).then_inc(att_p, 1)
            for n in range(2):
                pa = batch(dve, "xpv", n)
                drain_aux(dve.tensor_copy(AXo[:, 2 * n:2 * n + 2, :], v3(pa, 2)), "xpv", n)
                wait_aux(dve, "xpv", n)
                dve.engine_nop().then_inc(ax_op, 1)
            residual("xo")
            rms(3, HN)
            dve.wait_ge(rows2_in, 16)
            for m in range(MT):
                dve.scalar_tensor_tensor(out=HN[:, m, :], in0=XR[:, m, :], scalar=rst[:, m:m + 1],
                                         in1=LNR[:, 0, :], op0=ALU.mult, op1=ALU.mult
                                         ).then_inc(hn_ready, 1)
            for j in range(4):
                pa = batch(dve, "h4T", j)
                drain_aux(dve.tensor_copy(opB[:, 2 * j:2 * j + 2, :], v3(pa, 2)), "h4T", j)

            TOP_STEPS = [0]

            def top16(vals, idx, src, work, dynamic=None):
                st.then(dve.max(vals[:, 0:8], src))
                st.do(dve.max_index(idx[:, 0:8], vals[:, 0:8], src))
                st.then(dve.match_replace(work, vals[:, 0:8], src, LOWEST))
                st.then(dve.max(vals[:, 8:16], work))
                st.then(dve.max_index(idx[:, 8:16], vals[:, 8:16], work))

            def topk(it):
                n0, st.met = st.n, (small_in, 32)
                sc = SC[:, :, :, :].rearrange("p m (h q) n -> p (m h) (q n)", q=2)
                src = sc[:, it, :] if isinstance(it, int) else \
                    sc[:, bass.ds(it, 1), :].rearrange("p a b -> p (a b)")
                st.then(dve.tensor_copy(sS[:, :, :].rearrange("p a b -> p (a b)"), src))
                for q in range(2):
                    top16(tv[:, q, :], ti[:, q, :], sS[:, q, :], sW[:, 0:NK])
                st.then(dve.tensor_copy(tif[:, :, :], ti[:, :, :]))
                b16 = [P, 16, 16]
                col = lambda ap: ap.rearrange("p (a b) -> p a b", b=1).broadcast_to(b16)
                row = lambda ap: ap.rearrange("p (a b) -> p a b", a=1).broadcast_to(b16)
                st.then(dve.tensor_tensor(cand[:, :, :], col(tv[:, 0, :]), row(tv[:, 1, :]), ALU.add))
                top16(cv[:, :], cp[:, 0, :], cand[:, :, :].rearrange("p a b -> p (a b)"), sW[:, :])
                dve.tensor_scalar(gs[:, 0:1], cv[:, 0:1], -1.0, None, ALU.mult).then_inc(top_v, 1)
                st.then(dve.tensor_scalar(cp[:, 1, :], cp[:, 0, :], 15, None, ALU.bitwise_and))
                st.then(dve.tensor_scalar(cp[:, 0, :], cp[:, 0, :], 4, None, ALU.logical_shift_right))
                st.then(dve.tensor_copy(cpf[:, :, :], cp[:, :, :]))
                for q in range(2):
                    st.then(dve.tensor_tensor(eq[:, :, :], row(C("iota")), col(cpf[:, q, :]), ALU.is_equal))
                    st.then(dve.tensor_tensor(eq[:, :, :], eq[:, :, :], row(tif[:, q, :]), ALU.mult))
                    st.then(dve.tensor_reduce(ef[:, q, :], eq[:, :, :], AX, ALU.add))
                dst = IDX[:, it, :] if isinstance(it, int) else \
                    IDX[:, bass.ds(it, 1), :].rearrange("p a b -> p (a b)")
                dve.scalar_tensor_tensor(out=dst, in0=ef[:, 0, :], scalar=float(NK), in1=ef[:, 1, :],
                                         op0=ALU.mult, op1=ALU.add).then_inc(idx_ready, 1)
                dve.wait_ge(top_e, it + 1)
                st.then(dve.reciprocal(gs[:, 1:2], gs[:, 1:2]))
                gdst = GW[:, it, :] if isinstance(it, int) else \
                    GW[:, bass.ds(it, 1), :].rearrange("p a b -> p (a b)")
                st.then(dve.tensor_scalar(gdst, gx[:, :], gs[:, 1:2], None, ALU.mult))
                TOP_STEPS[0], st.met = st.n - n0, None

            wait_aux(dve, "psc", 6)
            wait_aux(dve, "psc", 7)
            wait_aux(dve, "h4T", 3)
            topk(0)
            per_topk = TOP_STEPS[0]

            def pass_(m, it, par):
                if not (isinstance(it, int) and it == 15):
                    topk(it + 1)
                for k in range(TOPK):
                    dve.wait_ge(rd_in[k % 8], it * 32 + 16 * (k // 8 + 1))
                    dve.tensor_tensor_reduce(
                        out=JUNK[:, :], in0=RD[k % 8][:, :], in1=HN[:, m, :], scale=1.0,
                        scalar=0.0, op0=ALU.mult, op1=ALU.add,
                        accum_out=dots[:, par, k:k + 1]).then_inc(dot_done, 1)
                    dve.wait_ge(dot_done, it * 16 + (k + 1))
                dve.wait_ge(gelu_done, it + 1)
                gate = GW[:, it, :] if isinstance(it, int) else \
                    GW[:, bass.ds(it, 1), :].rearrange("p a b -> p (a b)")
                dve.tensor_tensor(coef[:, par, :], act_d[:, par, :], gate, ALU.mult
                                  ).then_inc(coef_ready, 1)

            for m, trips in ((0, 4), (1, 3)):
                with st.loop(0, trips, 2 * per_topk) as i:
                    for par in range(2):
                        pass_(m, i * 2 + (8 * m + par), par)
            pass_(1, 14, 0)
            pass_(1, 15, 1)
            for m in range(MT):
                dve.wait_ge(up_done, 128 * (m + 1))
                dve.tensor_tensor(XR[:, m, :], XR[:, m, :],
                                  psum[:, 4 + 2 * m:6 + 2 * m, :].rearrange("p a b -> p (a b)"),
                                  ALU.add).then_inc(fin_x, 1)
                dve.wait_ge(fin_sq, m + 1)
                dve.tensor_scalar(rst[:, m:m + 1], ssq[:, m, 0:1], 1.0 / D, RMS_EPS, ALU.mult, ALU.add
                                  ).then_inc(fin_ms, 1)
                dve.wait_ge(fin_sd, m + 1)
                st.then(dve.reciprocal(rst[:, m:m + 1], rst[:, m:m + 1]))
                dve.scalar_tensor_tensor(out=YO[:, m, :], in0=XR[:, m, :], scalar=rst[:, m:m + 1],
                                         in1=LNR[:, 1, :], op0=ALU.mult, op1=ALU.mult
                                         ).then_inc(fin_y, 1)

        @block.gpsimd
        def _(pool):
            pool.wait_ge(gml_in, 64)
            pool.affine_select(out=WS[:, :, :], in_=WS[:, :, :], compare_op=ALU.is_ge, fill=0.0, base=0,
                               pattern=[[0, 8], [1, P]], channel_multiplier=-1).then_inc(ws_masked, 1)

            st = Steps(pool, pool_step)

            st.met = (gemm_done, UNIT["pq"] + 8)

            def take_indices(it, par):
                src = IDX[:, it, :] if isinstance(it, int) else \
                    IDX[:, bass.ds(it, 1), :].rearrange("p a b -> p (a b)")
                pool.wait_ge(idx_ready, it + 1)
                st.then(pool.tensor_copy(cur[:, par, :], src))

            def gather(dst, table, par, k, ready):
                pool.indirect_dma_start(
                    out=dst[:, :], out_offset=None, in_=table,
                    in_offset=bass.IndirectOffsetOnAxis(ap=cur[:, par, k:k + 1], axis=0)
                ).then_inc(ready, 16)

            def down_rows(it, par, k):
                if not (isinstance(it, int) and it == 0 and k < 8):
                    st.wait(dot_done, it * 16 + (k - 7))
                gather(RD[k % 8], w_down, par, k, rd_in[k % 8])

            def up_rows(it, par, k):
                if not (isinstance(it, int) and it == 0 and k < 8):
                    st.wait(up_done, it * 16 + (k - 7))
                gather(RU[k % 8], w_up, par, k, ru_in[k % 8])

            def both(it, par):
                take_indices(it + 1, (par + 1) % 3)
                for k in range(TOPK):
                    down_rows(it + 1, (par + 1) % 3, k)
                    up_rows(it, par, k)

            pool.wait_ge(gemm_done, UNIT["pq"] + 8)
            take_indices(0, 0)
            for k in range(TOPK):
                down_rows(0, 0, k)
            both(0, 0)
            with st.loop(0, 4, 3) as i:
                both(i * 3 + 1, 1)
                both(i * 3 + 2, 2)
                both(i * 3 + 3, 0)
            both(13, 1)
            both(14, 2)
            for k in range(TOPK):
                up_rows(15, 0, k)


def kernel(**inputs):
    import concourse.bacc as bacc
    from concourse.bass_utils import run_bass_kernel_spmd as run

    a = {k: np.asarray(v) for k, v in inputs.items()}

    def k1024(w):
        c = w.shape[1] // 256
        return w.reshape(8, P, c, 256).transpose(2, 1, 0, 3).reshape(c, P, 2048)

    def k512(w):
        return w.reshape(4, P, 2, 2, 256).transpose(2, 1, 3, 0, 4).reshape(2, P, 2048)

    w_in = a["w_in"][0]
    c = lambda n: slice(n * 1024, (n + 1) * 1024)
    q_, f_, i_, og_, pv_, ga_, gb_ = (w_in[:, c(n)] for n in range(7))
    w2 = a["w_in_2"][0]
    order = np.arange(512).reshape(2, 4, 2, 32).transpose(0, 2, 1, 3).reshape(-1)
    pieces = [
        k1024(f_), k1024(q_), k1024(i_), k1024(pv_), k1024(og_), k1024(ga_), k1024(gb_),
        a["w_pool"][0].reshape(4, 2, P, 256).transpose(2, 0, 1, 3).reshape(1, P, 2048),
        k1024(a["w_a"][0]), k1024(a["w_out"][0]), k1024(a["xa_w_kv_2"][0][:, :512]),
        k1024(a["w_up"][0]),
        a["w_down"][0].reshape(4, 8, P, 4, 256).transpose(3, 0, 2, 1, 4).reshape(16, P, 2048),
        k1024(a["xa_w_kv_2"][0][:, 512:]),
        k1024(w2[:, 0:512][:, order]), k1024(w2[:, 512:1024][:, order]), k1024(w2[:, 1024:1536]),
        k1024(w2[:, 1536:2048]), k1024(w2[:, 2048:2560]), k1024(w2[:, 2560:3584]),
        k1024(w2[:, 3584:4608]), k512(a["moba_w_proj_2"][0]), k512(a["gmlp_w_proj_2"][0]),
        k1024(a["w_out_2"][0]), k1024(a["xa_w_q_2"][0]), k512(a["xa_w_o_2"][0]),
        k1024(a["peer_w_q_2"][0]),
    ]
    weights = np.concatenate(pieces)
    assert weights.shape[0] == NBLOCKS
    col = lambda v: v.reshape(8, P).T
    vecs = np.concatenate([col(v) for v in (
        a["lb_logits"][0], a["lb_logits"][1], a["hgrn_norm_g"][0], a["pool_scale"][0], a["ln1_g"][0],
        a["ln1_b"][0], a["norm_mix_g_2"][0], a["norm_xa_g_2"][0], a["norm_mem_g_2"][0])], axis=1)

    s, t = np.arange(P)[:, None], np.arange(P)[None, :]
    con = np.zeros((P, NCON), np.float32)

    def put(n, v):
        o, k = CON[n]
        con[:, o:o + k] = v

    put("ident", np.eye(P))
    put("ones", 1.0)
    causal = np.where(t <= s, 0.0, NEG)
    put("amask", np.concatenate([causal, np.zeros((P, P)), causal], axis=1))
    put("cmask", ((s // CH == t // CH) & (s <= t)).astype(np.float32))
    freq = np.float32(10000.0) ** (-np.arange(32, dtype=np.float32) / np.float32(32))
    ang = np.arange(T, dtype=np.float32)[None, :] * freq[np.arange(P) % 32][:, None]
    put("cos", np.cos(ang.astype(np.float32)))
    put("sin", np.sin(ang.astype(np.float32)))
    put("invc", np.concatenate([1.0 / np.minimum(np.arange(16) + 1, 2 << g) for g in range(4)])[None])
    put("reset", (np.arange(T) % CH != 0).astype(np.float32)[None])
    put("even", (s // CH % 2 == 0).astype(np.float32))
    put("odd", (s // CH % 2 == 1).astype(np.float32))
    put("iota", np.arange(16)[None])

    pad = np.zeros(512, np.float32)
    rows = np.stack([a["ln1_g"][0], a["ln1_b"][0], a["ln2_g"][0], a["ln2_b"][0],
                     np.concatenate([a["gmlp_norm_g_2"][0], pad]), a["norm_ffn_g_2"][0], a["final_g_2"]])
    arrays = {
        "weights": weights, "vecs": vecs, "consts": con,
        "xT": a["x"][0].T.reshape(8, P, T).transpose(1, 0, 2), "x": a["x"][0], "mem": a["mem_2"][0],
        "rows": rows, "gws": a["gmlp_w_s_2"][0].transpose(2, 0, 1),
        "gbs": a["gmlp_b_s_2"][0].reshape(4, 2, P).transpose(1, 0, 2),
        "subkeys": a["peer_subkeys_2"][0].reshape(16, NK, P).transpose(2, 0, 1),
        "w_down": a["peer_w_down_2"][0], "w_up": a["peer_w_up_2"][0],
    }
    arrays = {k: np.ascontiguousarray(v) for k, v in arrays.items()}
    nc = bacc.Bacc("TRN2", target_bir_lowering=False, num_devices=1)
    args = [nc.dram_tensor(k, v.shape, F32, kind="ExternalInput").ap() for k, v in arrays.items()]
    args.append(nc.dram_tensor("out", (T, D), F32, kind="ExternalOutput").ap())
    build(nc, *args)
    r = run(nc, [arrays], core_ids=[0])
    return r.results[0]["out"].reshape(1, T, D)
```

```python
from contextlib import ExitStack

import numpy as np
import concourse.bass as bass
import concourse.mybir as mybir

P = 128
T = 256
MT = T // P
D = 1024
DC = D // P
HEADS = 8
CH = 16
NCH = T // CH
PAIR = 2 * CH
NPAIR = T // PAIR
FF = 4096
MH, MHD = 8, 64
XH, XHD = 4, 128
PH, NK, TOPK = 8, 128, 16
ALPHA = 2.0 ** 0.25
LN_EPS, RMS_EPS = 1e-5, 1e-6
NEG = -1e30
LOWEST = -3.0e38

F32 = mybir.dt.float32
F32R = mybir.dt.float32r
U32 = mybir.dt.uint32
ALU = mybir.AluOpType
ACT = mybir.ActivationFunctionType
AX = mybir.AxisListType.X

STAGES = [
    ("f", 4, 4), ("q", 4, 4), ("i", 4, 4), ("pv", 4, 4), ("og", 4, 4), ("ga", 4, 4), ("gb", 4, 4),
    ("pool", 1, 4), ("wa", 4, 4), ("wo", 4, 4), ("xka", 1, 1), ("up", 16, 16), ("down", 16, 4),
    ("xv", 2, 2), ("q2", 2, 2), ("k2", 2, 2), ("v2", 2, 2), ("gu", 2, 2), ("gv", 2, 2),
    ("ga2", 4, 4), ("gb2", 4, 4), ("ma", 2, 4), ("gm", 2, 4), ("wo2", 4, 4), ("xkb", 1, 1), ("xq", 2, 2),
    ("xo", 2, 4), ("pq", 8, 8),
]
BLOCK, RING, GROUPS = {}, {}, {}
_b = _r = 0
for _n, _nb, _ng in STAGES:
    BLOCK[_n], RING[_n], GROUPS[_n] = _b, _r, (_nb, _ng)
    _b, _r = _b + _nb, _r + _ng
NBLOCKS = _b


def half_end(b, h=1):
    return 2 * b + h + 1


def group_end(stage, j):
    nb, ng = GROUPS[stage]
    if ng < nb:
        return half_end(BLOCK[stage] + (nb // ng) * (j + 1) - 1)
    per = ng // nb
    return half_end(BLOCK[stage] + j // per, 1 if per == 1 else (j % per) * 2 // per)


SPLIT, _k = {}, 0
for _n, _p in [("x", 2), ("pooled", 4), ("o", 4), ("m", 4), ("mem", 4), ("ln1", 4), ("h", 16),
               ("h2", 4), ("at", 2), ("gm", 2), ("m2", 4), ("h3", 4), ("ax", 2), ("h4", 4)]:
    SPLIT[_n] = _k
    _k += _p

AUX = {}
_a = 0
for _n, _k in [("kT", 4), ("sc", 4), ("sx", 4), ("U", 2 * NPAIR - 2), ("osum", 1), ("obc", 4), ("memT", 4), ("ln1T", 4),
               ("h2T", 4), ("pv0", 1), ("pv1", 1), ("z", 2), ("h3T", 4), ("xpv", 2), ("h4T", 4),
               ("psc", 8)]:
    AUX[_n] = _a
    _a += _k

VEC = {n: 8 * i for i, n in enumerate(
    ["lb0", "lb1", "hg", "ps", "ln1g", "ln1b", "mixg", "xag", "memg", "ffng"])}
NVEC = 8 * len(VEC)
CON, _c = {}, 0
for _n, _k in [("ident", 128), ("ones", 128), ("amask", 384), ("cmask", 128), ("xmask", 128), ("cos", 256),
               ("sin", 256), ("invc", 64), ("reset", 256), ("iota", 16),
               ("zero", 1)]:
    CON[_n] = (_c, _k)
    _c += _k
NCON = _c


class Steps:

    def __init__(self, eng, sem):
        self.eng, self.sem, self.n, self.dyn = eng, sem, 0, 0
        self.met = None

    def do(self, ins):
        ins.then_inc(self.sem, 1)
        self.n += 1

    def sync(self):
        self.wait(self.sem, self.dyn + self.n)

    def wait(self, sem, value):
        if self.met and not isinstance(value, int):
            value = self.eng.to_reg(value)
            self.eng.wait_ge(*self.met)
        self.eng.wait_ge(sem, value)

    def then(self, ins):
        self.do(ins)
        self.sync()

    def loop(self, start, end, per):
        return _Loop(self, start, end, per)


class _Loop:
    def __init__(self, steps, start, end, per):
        self.s, self.a, self.b, self.per = steps, start, end, per

    def __enter__(self):
        self.cm = self.s.eng.Fori(self.a, self.b)
        i = self.cm.__enter__()
        self.n0 = self.s.n
        self.s.dyn = (i - self.a) * self.per if self.a else i * self.per
        return i

    def __exit__(self, *e):
        assert e[0] is not None or self.s.n - self.n0 == self.per, (self.s.n - self.n0, self.per)
        self.s.dyn = 0
        self.s.n = self.n0 + self.per * (self.b - self.a)
        return self.cm.__exit__(*e)


def build(nc, weights, vecs, consts, xT, x, mem, rows, gws, gbs, subkeys, w_down, w_up, out):
    ctx = ExitStack()
    with ctx:
        BASE = 16512
        SMALL = 16224
        UB = 8192
        at = [BASE]

        def small(name, shape, dt=F32):
            size = int(np.prod(shape[1:])) * 4
            t = nc.alloc_sbuf_tensor_at(name, shape, dt, offset=at[0])
            at[0] += (size + 31) // 32 * 32
            assert at[0] <= BASE + SMALL, (name, at[0] - BASE)
            return t

        def unit(name, u, shape, dt=F32, off=0):
            size = int(np.prod(shape[1:])) * 4
            o = BASE + SMALL + u * UB + off
            assert o + size <= BASE + SMALL + 24 * UB
            return nc.alloc_sbuf_tensor_at(name, shape, dt, offset=o)

        def sem(name):
            return ctx.enter_context(nc.semaphore(name))

        con = small("con", [P, NCON])
        vec = small("vec", [P, NVEC])

        def C(n):
            o, k = CON[n]
            return con[:, o:o + k]

        ident, ones = C("ident"), C("ones")
        raw = [unit(f"raw{s}", s, [P, DC, 256]) for s in range(4)]
        w_lo = [unit(f"w_lo{s}", s, [P, DC, 256], F32R) for s in range(4)]
        w_hi = [unit(f"w_hi{s}", 4 + s, [P, DC, 256], F32R) for s in range(4)]

        def pair(name, u, chunks, u2=None, off2=0):
            return (unit(name + "_hi", u, [P, chunks, T], F32R),
                    unit(name + "_lo", u + 1 if u2 is None else u2, [P, chunks, T], F32R, off=off2))

        opA, opB, opC = pair("opA", 8, DC), pair("opB", 10, DC), pair("opC", 12, DC)
        XF = unit("XF", 14, [P, DC, T])
        Q = unit("Q", 14, [P, HEADS, T])
        FK = unit("FK", 15, [P, HEADS, T])
        KE = unit("KE", 16, [P, HEADS, T])
        G = unit("G", 17, [P, HEADS, T])
        EG = unit("EG", 18, [P, HEADS, T])
        KI = unit("KI", 19, [P, HEADS, T])
        VN = unit("VN", 10, [P, MT, HEADS, P])
        KE2 = unit("KE2", 18, [P, HEADS, T])
        KN = unit("KN", 17, [P, MT, HEADS, P])
        PT = unit("PT", 20, [P, MT, HEADS, P])
        S = unit("S", 21, [P, 2, HEADS, P])
        SD = unit("SD", 15, [P, HEADS, P])
        OG = unit("OG", 22, [P, HEADS, T])
        PV = unit("PV", 23, [P, DC, T])
        sumA = unit("sumA", 12, [P, DC, T + 16])
        sumB = unit("sumB", 12, [P, 6, T + 16], off=8 * (T + 16) * 4)
        GA = unit("GA", 19, [P, DC, T])
        GB = unit("GB", 16, [P, DC, T])
        SQ = unit("SQ", 20, [P, HEADS, MT, P])
        DG = unit("DG", 17, [P, HEADS * MT, P])
        MB = unit("MB", 14, [P, DC, T])
        AM = unit("AM", 18, [P, 4, 2, T])
        MEM = unit("MEM", 21, [P, MT, D])
        XR = unit("XR", 23, [P, MT, D])
        LNR = unit("LNR", 22, [P, 2, D])
        HT = pair("HT", 14, FF // P, 18)
        RL = unit("RL", 9, [P, 2, 2, T])
        RQ = unit("RQ", 9, [P, 2, 2, T], off=4096)
        LT = unit("LT", 21, [P, 2, 2, T])
        KX = unit("KX", 8, [P, XH, T])
        VX = unit("VX", 8, [P, MT, XH * XHD], off=4096)
        XN = unit("XN", 21, [P, MT, D])
        GA2 = unit("GA2", 14, [P, DC, T])
        GB2 = unit("GB2", 15, [P, DC, T])
        QR = unit("QR", 16, [P, 2, 2, T])
        KR = unit("KR", 16, [P, 2, 2, T], off=4096)
        V2 = unit("V2", 17, [P, MT, 512])
        GU = unit("GU", 17, [P, 4, T], off=4096)
        GV = unit("GV", 18, [P, MT, 512])
        WS = unit("WS", 18, [P, 8, P], off=4096)
        R1 = unit("R1", 9, [P, 2, T])
        R2 = unit("R2", 9, [P, 2, T], off=2048)
        AS = unit("AS", 19, [P, 4, 384])
        ATT = unit("ATT", 20, [P, 4, 384])
        AT = pair("AT", 22, 4, 22, 4096)
        GM = pair("GM", 16, 4, 16, 4096)
        GR = unit("GR", 20, [P, 512], off=6144)
        BS = unit("BS", 19, [P, 4, P], off=6144)
        ZB = unit("ZB", 21, [P, 2, 2, MT, P])
        MA = unit("MA", 9, [P, DC, T])
        QX = unit("QX", 16, [P, XH, T])
        XS = unit("XS", 19, [P, XH * MT, T])
        XT = unit("XT", 20, [P, XH, 2, T])
        AXo = pair("AXo", 12, 4, 12, 4096)
        QP = unit("QP", 14, [P, 16, T])
        SK = unit("SK", 16, [P, 16, NK])
        SC = unit("SC", 17, [P, MT, 16, NK])
        RD = [unit(f"RD{s}", (8, 9, 12, 13)[s // 2], [P, D], off=4096 * (s % 2)) for s in range(8)]
        RU_AFTER = (NBLOCKS - 4, NBLOCKS - 4, NBLOCKS - 3, NBLOCKS - 3)
        RU = [unit(f"RU{s}", RU_AFTER[s // 2] % 4 + 4 * (s // 2 % 2), [P, D], off=4096 * (s % 2))
              for s in range(8)]
        BY_DVE = (9, 11, 13, 15)
        DIAG = unit("DIAG", 19, [P, TOPK, P])
        JUNK = unit("JUNK", 20, [P, D])
        YO = unit("YO", 14, [P, MT, D])

        lbd = small("lbd", [P, 16])
        lb = small("lb", [P, 8])
        lbx = small("lbx", [P, 8])
        DEC = small("DEC", [P, NCH, HEADS])
        st16 = small("st16", [P, 16])
        bst = small("bst", [P, MT, 4, 6])
        mv = small("mv", [P, MT, 2])
        rst = small("rst", [P, MT])
        ssq = small("ssq", [P, MT, 4])
        msq = small("msq", [P, MT])
        mrs = small("mrs", [P, MT])
        amx = small("amx", [P, 8])
        asm = small("asm", [P, 8])
        IDX = small("IDX", [P, 16, TOPK], U32)
        cur = small("cur", [P, 3, TOPK], U32)
        GW = small("GW", [P, 16, TOPK])
        dots = small("dots", [P, 2, TOPK])
        act_d = small("act_d", [P, 2, TOPK])
        coef = small("coef", [P, 2, TOPK])
        sS = small("sS", [P, 2, NK])
        sW = small("sW", [P, 256])
        cand = small("cand", [P, 16, 16])
        eq = unit("eq", 20, [P, 2, 16, 16], off=4096)
        tv = small("tv", [P, 2, 16])
        ti = small("ti", [P, 2, 16], U32)
        tif = small("tif", [P, 2, 16])
        cv = small("cv", [P, 16])
        cp = small("cp", [P, 2, 16], U32)
        cpf = small("cpf", [P, 2, 16])
        ef = small("ef", [P, 2, 16])
        gx = small("gx", [P, 16])
        gs = small("gs", [P, 2])

        psum = ctx.enter_context(nc.psum_tensor("ps", [P, 8, 512], F32))

        def bank(r):
            return psum[:, r % 2, :]

        def aux(a):
            return psum[:, 2 + a % 2, :]

        TURNED = ("ln1T", "h2T", "h3T", "h4T")

        def aux_bank(name, j):
            return psum[:, 2 + j, :] if name in TURNED and j >= 2 else aux(AUX[name] + j)

        raw_ready = [sem(f"raw_ready{s}") for s in range(4)]
        hi_ready, lo_ready = sem("hi_ready"), sem("lo_ready")
        split_hi, split_lo = sem("split_hi"), sem("split_lo")
        first_in, gemm_done = sem("first_in"), sem("gemm_done")
        drained = [sem(f"drained{s}") for s in range(2)]
        aux_done = sem("aux_done")
        aux_drained = [sem(f"aux_drained{s}") for s in range(2)]
        small_in, vec_in, x_in, xr_in, mem_in = sem("small_in"), sem("vec_in"), [sem("x_in0"), sem("x_in1")], sem("xr_in"), sem("mem_in")
        rows_in, gml_in, sk_in, rows2_in = (
            sem("rows_in"), sem("gml_in"), sem("sk_in"), sem("rows2_in"))
        dve_step, act_step, pool_step = sem("dve_step"), sem("act_step"), sem("pool_step")
        lb_diff, lb_exp = sem("lb_diff"), sem("lb_exp")
        f_ready, logf_ready, g_ready = sem("f_ready"), sem("logf_ready"), sem("g_ready")
        eg_ready, ki_exp, kd_ready, ke_exp = sem("eg_ready"), sem("ki_exp"), sem("kd_ready"), sem("ke_exp")
        hg_ready, ke2_ready, q2_ready = sem("hg_ready"), sem("ke2_ready"), sem("q2_ready")
        intra_done, o_done, sq_done, o_var, o_std = (
            sem("intra_done"), sem("o_done"), sem("sq_done"), sem("o_var"), sem("o_std"))
        diag_ready, o_ready, pooled_ready, m_ready = (
            sem("diag_ready"), sem("o_ready"), sem("pooled_ready"), sem("m_ready"))
        mem_sq, mem_ms, mem_sd, mem_z = sem("mem_sq"), sem("mem_ms"), sem("mem_sd"), sem("mem_z")
        ln_var, ln_std, ln_z, ln_op = sem("ln_var"), sem("ln_std"), sem("ln_z"), sem("ln_op")
        x_res = sem("x_res")
        rms_sq, rms_ms, rms_sd, rms_z, rms_rst = (
            sem("rms_sq"), sem("rms_ms"), sem("rms_sd"), sem("rms_z"), sem("rms_rst"))
        x_new = sem("x_new")
        quad_done, quad_read = sem("quad_done"), sem("quad_read")
        att_max, att_exp, att_p, att_t = sem("att_max"), sem("att_exp"), sem("att_p"), sem("att_t")
        gv_sq, gv_ms, gv_sd, gv_n, ws_masked, gm_ready = (
            sem("gv_sq"), sem("gv_ms"), sem("gv_sd"), sem("gv_n"), sem("ws_masked"), sem("gm_ready"))
        m2_ready = sem("m2_ready")
        top_v, top_e, idx_ready = sem("top_v"), sem("top_e"), sem("idx_ready")
        rd_in = [sem(f"rd_in{s}") for s in range(8)]
        ru_in = [sem(f"ru_in{s}") for s in range(8)]
        dot_done, gelu_done, coef_ready, dg_ready, up_done = (
            sem("dot_done"), sem("gelu_done"), sem("coef_ready"), sem("dg_ready"), sem("up_done"))
        fin_x, fin_sq, fin_ms, fin_sd, fin_y, stored = (
            sem("fin_x"), sem("fin_sq"), sem("fin_ms"), sem("fin_sd"), sem("fin_y"), sem("stored"))

        def group(eng, stage, j):
            eng.wait_ge(gemm_done, group_end(stage, j))
            return bank(RING[stage] + j)

        def drain(ins, stage, j):
            ins.then_inc(drained[(RING[stage] + j) % 2], 1)

        def wait_drained(eng, stage, j):
            r = RING[stage] + j
            eng.wait_ge(drained[r % 2], r // 2 + 2)

        def wait_stage(eng, stage, n):
            for j in range(max(0, n - 2), n):
                wait_drained(eng, stage, j)

        def has_hi(eng, name, j):
            eng.wait_ge(split_hi, SPLIT[name] + j + 1)

        def has_lo(eng, name, j):
            eng.wait_ge(split_lo, SPLIT[name] + j + 1)

        def two(op, j):
            return op[0][:, 2 * j:2 * j + 2, :], op[1][:, 2 * j:2 * j + 2, :]

        def batch(eng, name, j=0):
            a = AUX[name] + j
            eng.wait_ge(aux_done, a + 1)
            return aux_bank(name, j)

        def drain_aux(ins, name, j=0):
            ins.then_inc(aux_drained[(AUX[name] + j) % 2], 1)

        def wait_aux(eng, name, j=0):
            a = AUX[name] + j
            eng.wait_ge(aux_drained[a % 2], a // 2 + 1)

        def v3(ap, n):
            return ap.rearrange("p (a b) -> p a b", a=n)

        block = ctx.enter_context(nc.Block())

        @block.sync
        def _(sp):
            def load_x(h):
                sp.dma_start(XF[:, 4 * h:4 * h + 4, :], xT[:, 4 * h:4 * h + 4, :]).then_inc(x_in[h], 16)

            def load(b, s, after=None):
                if after is not None:
                    sp.wait_ge(gemm_done, after)
                sp.dma_start(raw[s][:, :, :].rearrange("p a b -> p (a b)"),
                             weights[b] if isinstance(b, int) else
                             weights[bass.ds(b, 1)].rearrange("a p n -> (a p) n")
                             ).then_inc(raw_ready[s], 16)

            load_x(0)
            half = DC // 2 * 256
            sp.dma_start(raw[0][:, 0:4, :].rearrange("p a b -> p (a b)"), weights[0][:, 0:half]
                         ).then_inc(first_in, 16)
            sp.dma_start(raw[0][:, 4:8, :].rearrange("p a b -> p (a b)"), weights[0][:, half:]
                         ).then_inc(raw_ready[0], 16)
            load_x(1)
            sp.dma_start(vec[:, :], vecs).then_inc(vec_in, 16)
            load(1, 1)
            sp.dma_start(con[:, :], consts).then_inc(small_in, 16)
            load(2, 2)
            load(3, 3)
            with sp.Fori(0, NBLOCKS // 4 - 1) as i:
                for s in range(4):
                    load(i * 4 + (4 + s), s, i * 8 + half_end(s))
            for b in range(NBLOCKS // 4 * 4, NBLOCKS):
                load(b, b % 4, half_end(b - 4))
            for m in range(MT):
                sp.wait_ge(fin_y, m + 1)
                sp.dma_start(out[m * P:(m + 1) * P, :], YO[:, m, :]).then_inc(stored, 16)
            sp.wait_ge(stored, 32)

        @block.tensor
        def _(pe):
            def take(s, ready):
                pe.wait_ge(lo_ready, ready)
                return w_hi[s], w_lo[s]

            def free_bank(r):
                pe.wait_ge(drained[r % 2], r // 2 + 1)

            def parts(w, op):
                return ((w[0], op[1]), (w[1], op[0]), (w[0], op[0]))

            def across(dst, w, op, ks, first=True, last=True, k0=0):
                for c in range(2):
                    for i in ks:
                        for n, (a, b) in enumerate(parts(w, op)):
                            mm = pe.matmul(dst[:, c * T:(c + 1) * T], a[:, i, c * P:(c + 1) * P],
                                           b[:, k0 + i, :],
                                           start=(first and c == 0 and i == ks[0] and n == 0),
                                           stop=(last and i == ks[-1] and n == 2),
                                           skip_group_check=True)
                return mm

            def down(dst, w, op, ks, first=True, last=True, k0=0):
                for m in range(MT):
                    for i in ks:
                        for n, (a, b) in enumerate(parts(w, op)):
                            mm = pe.matmul(dst[:, m * 256:(m + 1) * 256],
                                           b[:, k0 + i, m * P:(m + 1) * P], a[:, i, :],
                                           start=(first and m == 0 and i == ks[0] and n == 0),
                                           stop=(last and i == ks[-1] and n == 2),
                                           skip_group_check=True)
                return mm

            def halves_of(kind, dst, s, op, ready, need=None, first=True, last=True, k0=0, mid=None):
                for h in range(2):
                    if mid and h == 1:
                        mid()
                    w = take(s, ready + h)
                    if need:
                        has_lo(pe, *need[h])
                    kind(dst, w, op, range(4 * h, 4 * h + 4), first and h == 0, last and h == 1, k0
                         ).then_inc(gemm_done, 1)

            def one(stage, j, op, kind, need=None, mid=None):
                r, b = RING[stage] + j, BLOCK[stage] + j
                free_bank(r)
                halves_of(kind, bank(r), b % 4, op, half_end(b, 0), need, mid=mid)

            def first_of(name):
                return ((name, 1), (name, 3))

            def halves(stage, j, op, kind, need=None):
                b = BLOCK[stage] + j
                for h in range(2):
                    r = RING[stage] + 2 * j + h
                    w = take(b % 4, half_end(b, h))
                    if need and h == 0:
                        has_lo(pe, need, 1)
                    free_bank(r)
                    kind(bank(r), w, op, range(4 * h, 4 * h + 4), k0=-4 * h).then_inc(gemm_done, 1)

            def free_aux(name, j=0):
                a = AUX[name] + j
                if a >= 2 and not (name in TURNED and j >= 2):
                    pe.wait_ge(aux_drained[a % 2], a // 2)
                return aux_bank(name, j)

            def transposes(name, j, pieces):
                dst = free_aux(name, j)
                for n, src in enumerate(pieces):
                    mm = pe.transpose(dst[:, n * P:(n + 1) * P], src, ident)
                mm.then_inc(aux_done, 1)

            def to_across(name, src, j):
                transposes(name, j, [src[:, m, c * P:(c + 1) * P] for c in (2 * j, 2 * j + 1)
                                     for m in range(MT)])

            one("f", 0, opA, across, (("x", 0), ("x", 1)))
            for j in range(1, 4):
                one("f", j, opA, across)
            for j in range(4):
                one("q", j, opA, across)
            for j in range(4):
                one("i", j, opA, down)

            def ke_turn(n):
                m, q = n // 2, n % 2
                if n == 0:
                    pe.wait_ge(small_in, 16)
                    pe.wait_ge(ke2_ready, 1)
                transposes("kT", n, [KE2[:, 4 * q + h, m * P:(m + 1) * P] for h in range(4)])

            def scores(n):
                m, q = n // 2, n % 2
                dst = free_aux("sc", n)
                for h in range(4):
                    t = slice(m * P, (m + 1) * P)
                    mm = pe.matmul(dst[:, h * P:(h + 1) * P], KI[:, 4 * q + h, t], Q[:, 4 * q + h, t],
                                   start=True, stop=True)
                mm.then_inc(aux_done, 1)

            def cross(n):
                m, q = n // 2, n % 2
                dst = free_aux("sx", n)
                for h in range(4):
                    t = slice(m * P, (m + 1) * P)
                    mm = pe.matmul(dst[:, h * P:(h + 1) * P], KE[:, 4 * q + h, t], Q[:, 4 * q + h, t],
                                   start=True, stop=True)
                mm.then_inc(aux_done, 1)

            def intra(q):
                wait_stage(pe, "i", 4)
                wait_aux(pe, "sx", 2)
                wait_aux(pe, "sx", 3)
                for h in range(4 * q, 4 * q + 4):
                    dst = psum[:, 4 + h // 2, (h % 2) * T:(h % 2 + 1) * T]
                    for m in range(MT):
                        mm = pe.matmul(dst[:, m * P:(m + 1) * P], VN[:, m, h, :], PT[:, m, h, :],
                                       start=(h % 2 == 0 and m == 0), stop=True,
                                       skip_group_check=True)
                mm.then_inc(intra_done, 1)

            def before(c):
                if c == 1:
                    pe.wait_ge(q2_ready, 1)
                wait_aux(pe, "U", 2 * c - 2)
                wait_aux(pe, "U", 2 * c - 1)
                for h in range(HEADS):
                    t0 = (h % 2) * T + c * PAIR
                    mm = pe.matmul(psum[:, 4 + h // 2, t0:t0 + PAIR], S[:, c % 2, h, :],
                                   Q[:, h, c * PAIR:(c + 1) * PAIR], start=False, stop=True,
                                   skip_group_check=True)
                if c == NPAIR - 1:
                    mm.then_inc(o_done, 1)

            def adds(c):
                rows_ = slice(PAIR * (c % 4), PAIR * (c % 4) + PAIR)
                for half in range(2):
                    dst = free_aux("U", 2 * c + half)
                    for h in range(4):
                        mm = pe.matmul(dst[:, h * P:(h + 1) * P], KN[rows_, c // 4, 4 * half + h, :],
                                       VN[rows_, c // 4, 4 * half + h, :], start=True, stop=True)
                    mm.then_inc(aux_done, 1)

            one("pv", 0, opA, across)
            ke_turn(0)
            ke_turn(1)
            one("pv", 1, opA, across)
            ke_turn(2)
            ke_turn(3)
            one("pv", 2, opA, across)
            scores(0)
            scores(1)
            one("pv", 3, opA, across)
            scores(2)
            scores(3)
            one("og", 0, opA, across)
            cross(0)
            cross(1)
            one("og", 1, opA, across)
            cross(2)
            cross(3)
            one("og", 2, opA, across)
            intra(0)
            intra(1)
            adds(0)
            for n in range(1, NPAIR):
                st, j = [("og", 3), ("ga", 0), ("ga", 1), ("ga", 2), ("ga", 3), ("gb", 0),
                         ("gb", 1)][n - 1]
                one(st, j, opA, across, mid=lambda: before(n))
                if n < NPAIR - 1:
                    adds(n)
            one("gb", 2, opA, across)
            pe.wait_ge(sq_done, 1)
            dst = free_aux("osum")

            def head_sums(q):
                for n in range(8 * q, 8 * q + 8):
                    mm = pe.matmul(dst[:, n:n + 1], SQ[:, n // MT, n % MT, :], ones[:, 0:1],
                                   start=True, stop=True)
                return mm

            head_sums(0)
            one("gb", 3, opA, across, mid=lambda: head_sums(1).then_inc(aux_done, 1))

            def pool_groups(h):
                b = BLOCK["pool"]
                w = take(b % 4, half_end(b, h))
                for g in (2 * h, 2 * h + 1):
                    has_lo(pe, "pooled", g)
                    r = RING["pool"] + g
                    free_bank(r)
                    mm = across(bank(r), w, opB, range(2 * g, 2 * g + 2))
                mm.then_inc(gemm_done, 1)

            def rms_rows(j):
                dst = free_aux("obc", j)
                pe.matmul(dst, ones, DG[:, 4 * j:4 * j + 4, :].rearrange("p a b -> p (a b)"),
                          start=True, stop=True).then_inc(aux_done, 1)

            pool_groups(0)
            pe.wait_ge(diag_ready, 1)
            rms_rows(0)
            rms_rows(1)
            pool_groups(1)
            rms_rows(2)
            rms_rows(3)
            one("wa", 0, opC, across, first_of("o"))
            for j in range(1, 4):
                one("wa", j, opC, across)
            pe.wait_ge(mem_z, 1)
            to_across("memT", MEM, 0)
            to_across("memT", MEM, 1)
            one("wo", 0, opA, down, first_of("m"))
            one("wo", 1, opA, down)
            to_across("memT", MEM, 2)
            to_across("memT", MEM, 3)
            one("wo", 2, opA, down)
            one("wo", 3, opA, down)
            has_lo(pe, "mem", 3)
            one("xka", 0, opB, across)
            pe.wait_ge(ln_z, 1)
            for j in range(4):
                to_across("ln1T", XR, j)
            b0, r0 = BLOCK["up"], RING["up"]
            one("up", 0, opC, across, first_of("ln1"))
            for j in range(1, 4):
                one("up", j, opC, across)
            with pe.Fori(1, 4) as i:
                for s in range(4):
                    b, r = b0 + s, r0 + s
                    pe.wait_ge(drained[r % 2], i * 2 + (r // 2 + 1))
                    halves_of(across, bank(r), b % 4, opC, i * 8 + half_end(b, 0))
            for j in range(4):
                r = RING["down"] + j
                free_bank(r)
                for k in range(4):
                    b = BLOCK["down"] + 4 * j + k
                    need = (("h", 4 * k + 1), ("h", 4 * k + 3)) if j == 0 else None
                    halves_of(down, bank(r), b % 4, HT, half_end(b, 0), need, first=(k == 0),
                              last=(k == 3), k0=8 * k)
            for j in range(2):
                one("xv", j, opB, down)
            pe.wait_ge(rms_z, 2)
            for j in range(4):
                to_across("h2T", XN, j)
            one("q2", 0, opC, across, first_of("h2"))
            one("q2", 1, opC, across)
            for j in range(2):
                one("k2", j, opC, across)
            for j in range(2):
                one("v2", j, opC, down)

            def att_scores(a):
                if a == 0:
                    wait_stage(pe, "k2", 2)
                else:
                    pe.wait_ge(quad_read, 2)
                for part in range(2):
                    for h in range(4):
                        rw = slice(32 * h, 32 * h + 32)
                        dst = psum[:, 4 + h, :]
                        mm = pe.matmul(dst[:, 0:P], QR[rw, a, part, 0:P], KR[rw, a, part, 0:P],
                                       start=(part == 0), stop=(part == 1), skip_group_check=True)
                        mm = pe.matmul(dst[:, P:3 * P], QR[rw, a, part, P:T], KR[rw, a, part, :],
                                       start=False, stop=(part == 1), skip_group_check=True)
                mm.then_inc(quad_done, 1)

            def att_turn(a):
                pe.wait_ge(att_p, a + 1)
                for h in range(4):
                    for n in range(3):
                        mm = pe.transpose(psum[:, 4 + h, n * P:(n + 1) * P],
                                          AS[:, h, n * P:(n + 1) * P], ident)
                mm.then_inc(quad_done, 1)

            def att_values(a):
                pe.wait_ge(att_t, a + 1)
                if a == 0:
                    wait_stage(pe, "v2", 2)
                dst = free_aux(f"pv{a}")
                for h in range(4):
                    head = 4 * a + h
                    o = dst[64 * (head % 2):64 * (head % 2) + 64, (h // 2) * T:(h // 2 + 1) * T]
                    vs = slice(head * MHD, (head + 1) * MHD)
                    pe.matmul(o, V2[:, 0, vs], ATT[:, h, 0:T], start=True, stop=False,
                              skip_group_check=True)
                    mm = pe.matmul(o[:, P:T], V2[:, 1, vs], ATT[:, h, T:3 * P], start=False,
                                   stop=True, skip_group_check=True)
                mm.then_inc(aux_done, 1)

            def spatial(n):
                dst = free_aux("z", n)
                for c in range(2):
                    for m in range(MT):
                        for half in range(2):
                            g = 2 * (2 * n + c) + half
                            mm = pe.matmul(dst[64 * half:64 * half + 64,
                                               (c * MT + m) * P:(c * MT + m + 1) * P],
                                           GV[:, m, g * 64:(g + 1) * 64], WS[:, g, :],
                                           start=True, stop=True, skip_group_check=True)
                mm.then_inc(aux_done, 1)

            att_scores(0)
            for j in range(2):
                one("gu", j, opC, across)
            att_turn(0)
            one("gv", 0, opC, down)
            att_scores(1)
            one("gv", 1, opC, down)
            att_values(0)
            one("ga2", 0, opC, across)
            one("ga2", 1, opC, across)
            att_turn(1)
            one("ga2", 2, opC, across)
            att_values(1)
            one("ga2", 3, opC, across)
            one("gb2", 0, opC, across)
            one("gb2", 1, opC, across)
            pe.wait_ge(gv_n, 2)
            pe.wait_ge(ws_masked, 1)
            spatial(0)
            spatial(1)
            one("gb2", 2, opC, across)
            one("gb2", 3, opC, across)
            for j in range(2):
                halves("ma", j, AT, across, "at")
            for j in range(2):
                halves("gm", j, GM, across, "gm")
            one("wo2", 0, opC, down, first_of("m2"))
            for j in range(1, 4):
                one("wo2", j, opC, down)
            one("xkb", 0, opB, across)
            pe.wait_ge(rms_z, 4)
            for j in range(4):
                to_across("h3T", XN, j)
            one("xq", 0, opB, across, first_of("h3"))
            one("xq", 1, opB, across)
            wait_stage(pe, "xq", 2)
            wait_drained(pe, "xka", 0)
            wait_drained(pe, "xkb", 0)
            for h in range(XH):
                for m in range(MT):
                    mm = pe.matmul(psum[:, 4 + h, m * T:(m + 1) * T], QX[:, h, m * P:(m + 1) * P],
                                   KX[:, h, :], start=True, stop=True)
                if h % 2:
                    mm.then_inc(quad_done, 1)
            wait_stage(pe, "xv", 2)
            for n in range(2):
                pe.wait_ge(att_p, 3 + n)
                for h in (2 * n, 2 * n + 1):
                    for s in range(2):
                        for m in range(MT):
                            mm = pe.transpose(psum[:, 4 + h, (s * MT + m) * P:(s * MT + m + 1) * P],
                                              XS[:, h * MT + m, s * P:(s + 1) * P], ident)
                mm.then_inc(quad_done, 1)
            for n in range(2):
                pe.wait_ge(att_t, 3 + n)
                dst = free_aux("xpv", n)
                for hh in range(2):
                    h = 2 * n + hh
                    for s in range(2):
                        mm = pe.matmul(dst[:, hh * T:(hh + 1) * T], VX[:, s, h * P:(h + 1) * P],
                                       XT[:, h, s, :], start=(s == 0), stop=(s == 1))
                mm.then_inc(aux_done, 1)
            for j in range(2):
                halves("xo", j, AXo, down, "ax")
            pe.wait_ge(rms_z, 6)
            for j in range(4):
                to_across("h4T", XN, j)
            def head_scores(j):
                wait_drained(pe, "pq", j)
                if j == 0:
                    pe.wait_ge(sk_in, 16)
                dst = free_aux("psc", j)
                for m in range(MT):
                    for c in (2 * j, 2 * j + 1):
                        k = m * 2 + c - 2 * j
                        mm = pe.matmul(dst[:, k * P:(k + 1) * P], QP[:, c, m * P:(m + 1) * P],
                                       SK[:, c, :], start=True, stop=True)
                mm.then_inc(aux_done, 1)

            one("pq", 0, opB, across, first_of("h4"))
            head_scores(0)
            one("pq", 1, opB, across)
            for j in range(2, 8):
                one("pq", j, opB, across, mid=lambda: head_scores(j - 1))
            head_scores(7)
            for m in range(MT):
                for n in range(2):
                    pe.matmul(psum[:, 4 + 2 * m + n, :], C("zero").broadcast_to([P, P]),
                              SK[:, 0:4, :].rearrange("p a b -> p (a b)"), start=True, stop=False,
                              skip_group_check=True)

                def pass_sum(m, it, picks):
                    for k in picks:
                        if k % 8 == 0:
                            pe.wait_ge(dg_ready, it * 2 + (k // 8 + 1))
                        pe.wait_ge(ru_in[k % 8], it * 32 + 16 * (k // 8 + 1))
                        for n in range(2):
                            mm = pe.matmul(psum[:, 4 + 2 * m + n, :], DIAG[:, k, :],
                                           RU[k % 8][:, n * 512:(n + 1) * 512], start=False,
                                           stop=True, skip_group_check=True)
                        mm.then_inc(up_done, 1)

                with pe.Fori(0, 8 if m == 0 else 7) as h:
                    pass_sum(m, h + 8 * m, range(TOPK))
            pass_sum(1, 15, [k for k in range(TOPK) if k not in BY_DVE])

        @block.scalar
        def _(act):
            st = Steps(act, act_step)

            def upper(s, in_at, first=False):
                for h in range(2):
                    if h or not first:
                        act.wait_ge(raw_ready[s], in_at)
                    else:
                        act.wait_ge(first_in, 16)
                    act.activation(w_hi[s][:, 4 * h:4 * h + 4, :], raw[s][:, 4 * h:4 * h + 4, :],
                                   ACT.Copy).then_inc(hi_ready, 1)

            split_to = [-1]

            def ahead(b):
                while split_to[0] < min(b, NBLOCKS - 1):
                    split_to[0] += 1
                    upper(split_to[0] % 4, 16 * (split_to[0] // 4 + 1), split_to[0] == 0)

            def evac(stage, j, dst, func, further=True):
                pb = group(act, stage, j)
                drain(act.activation(dst, v3(pb, 2), func), stage, j)
                if further:
                    ahead(BLOCK[stage] + j + 3)

            def hi_of(j, src, op):
                act.activation(two(op, j)[0], src, ACT.Copy).then_inc(split_hi, 1)

            def hi_turned(name, j, op, gain=None):
                pa = batch(act, name, j)
                if gain is None:
                    return act.activation(two(op, j)[0], v3(pa, 2), ACT.Copy).then_inc(split_hi, 1)
                for c in (2 * j, 2 * j + 1):
                    g = vec[:, VEC[gain] + c:VEC[gain] + c + 1]
                    src = pa[:, (c % 2) * T:(c % 2 + 1) * T]
                    ins = act.activation(op[0][:, c, :], src, ACT.Copy, scale=g)
                    if c % 2 == 0:
                        st.do(ins)
                ins.then_inc(split_hi, 1)

            ahead(1)
            act.wait_ge(lb_diff, 1)
            act.activation(lbd[:, :], lbd[:, :], ACT.Exp).then_inc(lb_exp, 1)
            ahead(2)
            for j in range(4):
                evac("f", j, FK[:, 2 * j:2 * j + 2, :], ACT.Sigmoid)
            for j in range(4):
                evac("q", j, Q[:, 2 * j:2 * j + 2, :], ACT.Silu)
            act.wait_ge(f_ready, 1)
            act.activation(KE[:, :, :], FK[:, :, :], ACT.Ln).then_inc(logf_ready, 1)
            ahead(11)
            act.wait_ge(g_ready, 1)
            act.activation(EG[:, :, :], G[:, :, :], ACT.Exp).then_inc(eg_ready, 1)
            act.activation(KI[:, :, :], G[:, :, :], ACT.Exp, scale=-1.0).then_inc(ki_exp, 1)
            ahead(12)
            act.wait_ge(kd_ready, 1)
            act.activation(KE[:, :, :], KE[:, :, :], ACT.Exp).then_inc(ke_exp, 1)
            ahead(14)
            for j in range(4):
                evac("pv", j, PV[:, 2 * j:2 * j + 2, :], ACT.Copy)
                for n in (2 * j, 2 * j + 1) if j < 2 else ():
                    pa = batch(act, "kT", n)
                    drain_aux(act.activation(KN[:, n // 2, 4 * (n % 2):4 * (n % 2) + 4, :], v3(pa, 4),
                                             ACT.Copy), "kT", n)

            def after_chunks():
                act.wait_ge(o_done, 1)
                act.activation(SQ[:, :, :, :].rearrange("p h m t -> p (h m t)"),
                               psum[:, 4:8, :].rearrange("p a b -> p (a b)"), ACT.Square
                               ).then_inc(sq_done, 1)
                act.dma_start(MEM[:, :, :], mem.rearrange("(m p) d -> p m d", p=P)).then_inc(mem_in, 16)
                for g in range(4):
                    act.wait_ge(pooled_ready, g + 1)
                    hi_of(g, PV[:, 2 * g:2 * g + 2, :], opB)

            for st_, dst in (("og", OG), ("ga", GA), ("gb", GB)):
                if st_ == "ga":
                    wait_aux(act, "sx", 2)
                    wait_aux(act, "sx", 3)
                for j in range(4):
                    evac(st_, j, dst[:, 2 * j:2 * j + 2, :], ACT.Sigmoid)
                    if (st_, j) == ("gb", 1):
                        after_chunks()
                    if (st_, j) == ("gb", 2):
                        act.wait_ge(o_var, 1)
                        act.activation(st16[:, :], st16[:, :], ACT.Sqrt).then_inc(o_std, 1)
                        has_lo(act, "pooled", 3)
                        act.dma_start(XR[:, :, :], x.rearrange("(m p) d -> p m d", p=P)
                                      ).then_inc(xr_in, 16)
            act.wait_ge(mem_in, 16)
            act.wait_ge(diag_ready, 1)
            for m in range(MT):
                st.do(act.activation(SQ[:, 4 * m:4 * m + 4, :, :].rearrange("p a b c -> p (a b c)"),
                                     MEM[:, m, :], ACT.Square, accum_out=msq[:, m:m + 1]))
            for j in range(4):
                act.wait_ge(o_ready, j + 1)
                hi_of(j, OG[:, 2 * j:2 * j + 2, :], opC)
            ahead(31)
            st.sync()
            act.activation(mrs[:, :], msq[:, :], ACT.Copy).then_inc(mem_sq, 1)
            act.wait_ge(mem_ms, 1)
            act.activation(mrs[:, :], mrs[:, :], ACT.Sqrt).then_inc(mem_sd, 1)
            act.dma_start(LNR[:, :, :], rows[0:2, :].partition_broadcast(P)).then_inc(rows_in, 16)
            for j in range(4):
                ahead(31 + j)
                act.wait_ge(m_ready, j + 1)
                hi_of(j, AM[:, j], opA)
            for j in range(4):
                hi_turned("memT", j, opB, "memg")
                ahead(35 + j // 2)
            ahead(BLOCK["wo"] + 5)
            act.wait_ge(ln_var, 1)
            act.activation(rst[:, :], rst[:, :], ACT.Sqrt).then_inc(ln_std, 1)
            ahead(BLOCK["wo"] + 6)
            evac("xka", 0, KX[:, 0:2, :], ACT.Copy, further=False)
            for j in range(4):
                act.wait_ge(ln_op, j + 1)
                hi_of(j, LT[:, j % 2], opC)
                if j == 1:
                    ahead(BLOCK["up"] + 2)
            r0, b0 = RING["up"], BLOCK["up"]
            with act.Fori(0, 4) as i:
                for s in range(4):
                    act.wait_ge(gemm_done, i * 8 + half_end(b0 + s))
                    act.wait_ge(split_lo, i * 4 + (SPLIT["h"] + s - 1))
                    act.activation(RL[:, s % 2], v3(bank(r0 + s), 2), ACT.Relu
                                   ).then_inc(drained[(r0 + s) % 2], 1)
                    act.wait_ge(drained[(r0 + s) % 2], i * 2 + ((r0 + s) // 2 + 2))
                    act.activation(HT[0][:, bass.ds(i * 8 + 2 * s, 2), :], RL[:, s % 2], ACT.Square
                                   ).then_inc(split_hi, 1)
                    b = b0 + s + 3
                    upper(b % 4, i * 16 + 16 * (b // 4 + 1))
            split_to[0] += 16
            ahead(BLOCK["down"] + 4)
            act.wait_ge(x_res, 2)
            act.dma_start(LNR[:, :, :], rows[2:4, :].partition_broadcast(P)).then_inc(rows_in, 16)
            ahead(BLOCK["xv"] + 1)
            act.wait_ge(ln_var, 2)
            act.activation(rst[:, :], rst[:, :], ACT.Sqrt).then_inc(ln_std, 1)

            def warm(func):
                st.then(act.activation(lbd[:, 2:3], C("zero"), func))

            def root(n):
                act.wait_ge(rms_ms, n)
                act.activation(rst[:, :], rst[:, :], ACT.Sqrt).then_inc(rms_sd, 1)

            def scaled(n):
                act.wait_ge(rms_rst, n)
                act.activation(XN[:, 1, :], XR[:, 1, :], ACT.Copy, scale=rst[:, 1:2]).then_inc(rms_z, 1)

            def squares_by_group(n, dst, stage):
                warm(ACT.Sqrt)
                for j in range(4):
                    act.wait_ge(x_new, 4 * n - 6 + j + 1)
                    for m in range(MT):
                        ins = act.activation(dst[:, m, 256 * j:256 * j + 256],
                                             XR[:, m, 256 * j:256 * j + 256], ACT.Square,
                                             accum_out=ssq[:, m, j:j + 1])
                        if (j, m) != (3, 1):
                            st.do(ins)
                    if j < 3 and stage == "wo2":
                        ahead(BLOCK[stage] + j + 3)
                ins.then_inc(rms_sq, 1)
                root(n)
                scaled(n)

            act.wait_ge(gemm_done, group_end("down", 3))
            act.dma_start(GR[:, :], rows[4:5, 0:512].rearrange("a n -> (a n)").partition_broadcast(P)
                          ).then_inc(gml_in, 16)
            act.dma_start(WS[:, :, :], gws).then_inc(gml_in, 16)
            act.dma_start(BS[0:64, :, :], gbs[0].partition_broadcast(64)).then_inc(gml_in, 16)
            act.dma_start(BS[64:128, :, :], gbs[1].partition_broadcast(64)).then_inc(gml_in, 16)
            ahead(BLOCK["q2"])
            for m in range(MT):
                act.wait_ge(x_new, m + 1)
                ins = act.activation(XN[:, m, :], XR[:, m, :], ACT.Square, accum_out=ssq[:, m, 0:1])
                if m == 0:
                    st.do(ins)
            ins.then_inc(rms_sq, 1)
            root(1)
            scaled(1)
            for j in range(2):
                evac("xv", j, VX[:, :, 256 * j:256 * j + 256], ACT.Copy, further=False)
            for j in range(4):
                hi_turned("h2T", j, opC, "mixg")
                if j == 1:
                    ahead(BLOCK["q2"] + 1)
            ahead(BLOCK["q2"] + 2)
            ahead(BLOCK["v2"] + 1)
            for j in range(2):
                evac("v2", j, V2[:, :, 256 * j:256 * j + 256], ACT.Copy)

            def exps(a):
                act.wait_ge(att_max, a + 1)
                for h in range(4):
                    for m in range(MT):
                        sl = slice(0, P) if m == 0 else slice(P, 3 * P)
                        ins = act.activation(AS[:, h, sl], AS[:, h, sl], ACT.Exp,
                                             bias=amx[:, 2 * h + m:2 * h + m + 1],
                                             accum_out=asm[:, 2 * h + m:2 * h + m + 1])
                        if (h, m) != (3, 1):
                            st.do(ins)
                ins.then_inc(att_exp, 1)

            def turned(a, n, src, dst):
                act.wait_ge(quad_done, n)
                act.activation(dst, src, ACT.Copy).then_inc(att_t, 1)

            warm(ACT.Exp)
            exps(0)
            for j in range(2):
                evac("gu", j, GU[:, 2 * j:2 * j + 2, :], ACT.Gelu_apprx_tanh)
            turned(0, 2, psum[:, 4:8, 0:384], ATT[:, :, :])
            for j in range(2):
                evac("gv", j, GV[:, :, 256 * j:256 * j + 256], ACT.Gelu_apprx_tanh)
            exps(1)
            hi_turned("pv0", 0, AT)
            wait_stage(act, "gv", 2)
            for m in range(MT):
                ins = act.activation(ZB[:, 0].rearrange("p a b c -> p (a b c)"), GV[:, m, :],
                                     ACT.Square, accum_out=ssq[:, m, 1:2])
                if m == 0:
                    st.then(ins)
            ins.then_inc(gv_sq, 1)
            act.wait_ge(gv_ms, 1)
            act.activation(ssq[:, :, 2], ssq[:, :, 2], ACT.Sqrt).then_inc(gv_sd, 1)
            for j in range(2):
                evac("ga2", j, GA2[:, 2 * j:2 * j + 2, :], ACT.Sigmoid)
            turned(1, 4, psum[:, 4:8, 0:384], ATT[:, :, :])
            for j in range(2, 4):
                evac("ga2", j, GA2[:, 2 * j:2 * j + 2, :], ACT.Sigmoid)
            hi_of(1, v3(batch(act, "pv1"), 2), AT)
            for j in range(4):
                evac("gb2", j, GB2[:, 2 * j:2 * j + 2, :], ACT.Sigmoid)
                if j == 2:
                    for n in range(2):
                        act.wait_ge(gm_ready, n + 1)
                        hi_of(n, ZB[:, n].rearrange("p c m t -> p c (m t)"), GM)
            ahead(BLOCK["gm"] + 1)
            for j in range(4):
                act.wait_ge(m2_ready, j + 1)
                hi_of(j, AM[:, j], opC)
                if j:
                    ahead(BLOCK["wo2"] + j - 1)
            squares_by_group(2, XN, "wo2")
            ahead(BLOCK["xq"] + 1)
            evac("xkb", 0, KX[:, 2:4, :], ACT.Copy, further=False)
            for j in range(4):
                hi_turned("h3T", j, opB, "xag")
                if j == 1:
                    ahead(BLOCK["xo"])
            for j in range(2):
                evac("xq", j, QX[:, 2 * j:2 * j + 2, :], ACT.Copy)
            warm(ACT.Exp)
            for n in range(2):
                act.wait_ge(att_max, 3 + n)
                for i in range(4 * n, 4 * n + 4):
                    h, m = i // 2, i % 2
                    ins = act.activation(XS[:, i, :], psum[:, 4 + h, m * T:(m + 1) * T], ACT.Exp,
                                         bias=amx[:, i:i + 1], scale=float(XHD) ** -0.5,
                                         accum_out=asm[:, i:i + 1])
                    if i < 4 * n + 3:
                        st.do(ins)
                ins.then_inc(att_exp, 1)
            for n in range(2):
                turned(2 + n, 7 + n, psum[:, 4 + 2 * n:6 + 2 * n, :],
                       XT[:, 2 * n:2 * n + 2].rearrange("p h s t -> p h (s t)"))
            act.dma_start(SK[:, :, :], subkeys).then_inc(sk_in, 16)
            for n in range(2):
                hi_turned("xpv", n, AXo)
            ahead(BLOCK["xo"] + 3)
            act.wait_ge(x_new, 7)
            act.dma_start(LNR[:, :, :], rows[5:7, :].partition_broadcast(P)).then_inc(rows2_in, 16)
            squares_by_group(3, XN, "xo")
            for j in range(4):
                hi_turned("h4T", j, opB, "ffng")
                if j % 2:
                    ahead(BLOCK["pq"] + 2 + j // 2)

            def head_scores(j):
                pa = batch(act, "psc", j)
                drain_aux(act.activation(SC[:, :, 2 * j:2 * j + 2, :].rearrange(
                    "p m q n -> p m (q n)"), v3(pa, 2), ACT.Copy), "psc", j)

            def gate_exp(it):
                act.wait_ge(top_v, it + 1)
                act.activation(gx[:, :], cv[:, :], ACT.Exp, bias=gs[:, 0:1],
                               accum_out=gs[:, 1:2]).then_inc(top_e, 1)

            def pass_(it, par):
                if not (isinstance(it, int) and it in (0, 15)):
                    gate_exp(it + 1)
                act.wait_ge(dot_done, it * 16 + 16)
                act.activation(act_d[:, par, :], dots[:, par, :], ACT.Gelu_apprx_tanh
                               ).then_inc(gelu_done, 1)
                act.wait_ge(coef_ready, it + 1)
                for k in range(TOPK):
                    if k % 8 == 0 and not (isinstance(it, int) and it == 0):
                        act.wait_ge(up_done, it * 16 + (k - 8))
                    ins = act.activation(DIAG[:, k, :], ident, ACT.Copy, scale=coef[:, par, k:k + 1])
                    if k % 8 == 7:
                        ins.then_inc(dg_ready, 1)

            for j in range(8):
                pb = group(act, "pq", j)
                drain(act.activation(QP[:, 2 * j:2 * j + 2, :], v3(pb, 2), ACT.Copy), "pq", j)
                head_scores(j)
                ahead(BLOCK["pq"] + j + 4)
                if j in (1, 3):
                    gate_exp(j // 2)
            pass_(0, 0)
            pass_(1, 1)
            with act.Fori(1, 7) as i:
                pass_(i * 2, 0)
                pass_(i * 2 + 1, 1)

            def last_norm(m):
                act.wait_ge(fin_x, m + 1)
                act.activation(YO[:, m, :], XR[:, m, :], ACT.Square, accum_out=ssq[:, m, 0:1]
                               ).then_inc(fin_sq, 1)
                act.wait_ge(fin_ms, m + 1)
                act.activation(rst[:, m:m + 1], rst[:, m:m + 1], ACT.Sqrt).then_inc(fin_sd, 1)

            pass_(14, 0)
            pass_(15, 1)
            last_norm(0)
            last_norm(1)

        @block.vector
        def _(dve):
            st = Steps(dve, dve_step)
            for s in range(2):
                dve.engine_nop().then_inc(drained[s], 1)

            def lower(j, src, op, name):
                has_hi(dve, name, j)
                hi, lo = two(op, j)
                return dve.tensor_tensor(lo, src, hi, ALU.subtract)

            def lo_of(j, src, op, name):
                lower(j, src, op, name).then_inc(split_lo, 1)

            def lo_drained(name, batch_, jb):
                wait_aux(dve, batch_, jb)
                dve.engine_nop().then_inc(split_lo, 1)

            def lo_turned(name, batch_, j, op, gain=None):
                pa = batch(dve, batch_, j)
                if gain is None:
                    ins = lower(j, v3(pa, 2), op, name)
                else:
                    has_hi(dve, name, j)
                    for c in (2 * j, 2 * j + 1):
                        ins = dve.scalar_tensor_tensor(
                            out=op[1][:, c, :], in0=pa[:, (c % 2) * T:(c % 2 + 1) * T],
                            scalar=V(gain, c), in1=op[0][:, c, :], op0=ALU.mult, op1=ALU.subtract)
                        if c % 2 == 0:
                            st.do(ins)
                drain_aux(ins, batch_, j)
                lo_drained(name, batch_, j)

            for h in range(2):
                ks = slice(4 * h, 4 * h + 4)
                dve.wait_ge(x_in[h], 16)
                dve.tensor_copy(opA[0][:, ks, :], XF[:, ks, :]).then_inc(split_hi, 1)
                dve.wait_ge(split_hi, h + 1)
                dve.tensor_tensor(opA[1][:, ks, :], XF[:, ks, :], opA[0][:, ks, :], ALU.subtract
                                  ).then_inc(split_lo, 1)
                if h == 0:
                    dve.wait_ge(hi_ready, 1)
                    dve.tensor_tensor(w_lo[0][:, ks, :], raw[0][:, ks, :], w_hi[0][:, ks, :],
                                      ALU.subtract).then_inc(lo_ready, 1)
            st.do(dve.memset(PT[:, :, :, :], 0.0))
            dve.wait_ge(vec_in, 16)
            V = lambda n, c: vec[:, VEC[n] + c:VEC[n] + c + 1]
            l0, l1 = vec[:, VEC["lb0"]:VEC["lb0"] + 8], vec[:, VEC["lb1"]:VEC["lb1"] + 8]
            st.then(dve.tensor_tensor(lbx[:, :], l0, l1, ALU.max))
            st.do(dve.tensor_tensor(lbd[:, 0:8], l0, lbx[:, :], ALU.subtract))
            dve.tensor_tensor(lbd[:, 8:16], l1, lbx[:, :], ALU.subtract).then_inc(lb_diff, 1)
            dve.wait_ge(lb_exp, 1)
            st.then(dve.tensor_tensor(lb[:, :], lbd[:, 0:8], lbd[:, 8:16], ALU.add))
            st.then(dve.reciprocal(lb[:, :], lb[:, :]))
            st.then(dve.tensor_tensor(lb[:, :], lb[:, :], lbd[:, 0:8], ALU.mult))
            st.then(dve.tensor_scalar(lbx[:, :], lb[:, :], -1.0, 1.0, ALU.mult, ALU.add))
            for j in range(4):
                wait_drained(dve, "f", j)
                for h in (2 * j, 2 * j + 1):
                    ins = dve.tensor_scalar(FK[:, h, :], FK[:, h, :], lbx[:, h:h + 1], lb[:, h:h + 1],
                                            ALU.mult, ALU.add)
                    if h < 7:
                        st.do(ins)
            ins.then_inc(f_ready, 1)
            dve.wait_ge(logf_ready, 1)
            dve.wait_ge(small_in, 16)

            def values(j):
                pb = group(dve, "i", j)
                drain(dve.tensor_copy(VN[:, :, 2 * j:2 * j + 2, :].rearrange("p m h v -> p m (h v)"),
                                      v3(pb, 2)), "i", j)

            for h in range(HEADS):
                ins = dve.tensor_tensor_scan(G[:, h, :], C("reset"), KE[:, h, :], 0.0, ALU.mult, ALU.add)
                if h < 7:
                    st.do(ins)
            ins.then_inc(g_ready, 1)
            values(0)
            st.then(dve.tensor_scalar(FK[:, :, :], FK[:, :, :], -1.0, 1.0, ALU.mult, ALU.add))
            dve.wait_ge(g_ready, 1)
            g4 = G[:, :, :].rearrange("p h (c s) -> p (h c) s", s=CH)
            ke4 = KE[:, :, :].rearrange("p h (c s) -> p (h c) s", s=CH)
            dve.tensor_tensor(ke4, g4[:, :, CH - 1:CH].broadcast_to([P, HEADS * NCH, CH]), g4,
                              ALU.subtract).then_inc(kd_ready, 1)
            values(1)
            dve.wait_ge(eg_ready, 1)
            st.do(dve.tensor_copy(DEC[:, :, :].rearrange("p c h -> p h c"),
                                  EG[:, :, :].rearrange("p h (c s) -> p h c s", s=CH)[:, :, :, CH - 1]))
            wait_stage(dve, "q", 4)
            dve.scalar_tensor_tensor(out=Q[:, :, :], in0=Q[:, :, :], scalar=float(P) ** -0.5,
                                     in1=EG[:, :, :], op0=ALU.mult, op1=ALU.mult).then_inc(hg_ready, 1)
            dve.wait_ge(ki_exp, 1)
            dve.tensor_tensor(KI[:, :, :], KI[:, :, :], FK[:, :, :], ALU.mult).then_inc(hg_ready, 1)
            dve.wait_ge(ke_exp, 1)
            dve.tensor_tensor(KE[:, :, :], KE[:, :, :], FK[:, :, :], ALU.mult).then_inc(hg_ready, 1)
            dve.wait_ge(hg_ready, 3)
            pairs = lambda x: x.rearrange("p h (c u s) -> p h c u s", u=2, s=CH)
            dec = DEC[:, :, :].rearrange("p (c u) h -> p u h c", u=2)

            def decay(u, q):
                return dec[:, u, 4 * q:4 * q + 4, :].rearrange("p h (c s) -> p h c s", s=1
                                                               ).broadcast_to([P, 4, NPAIR, CH])

            values(2)
            for q in range(2):
                hs = slice(4 * q, 4 * q + 4)
                st.do(dve.tensor_tensor(pairs(KE2[:, hs])[:, :, :, 0, :], pairs(KE[:, hs])[:, :, :, 0, :],
                                        decay(1, q), ALU.mult))
            dve.tensor_copy(pairs(KE2[:, :, :])[:, :, :, 1, :].rearrange("p h c s -> p (h c) s"),
                            pairs(KE[:, :, :])[:, :, :, 1, :].rearrange("p h c s -> p (h c) s")
                            ).then_inc(ke2_ready, 1)
            values(3)
            st.then(dve.memset(SD[:, :, :], 0.0))
            cm, xm = C("cmask").bitcast(U32), C("xmask").bitcast(U32)

            def masked(name, j, mask):
                pa = batch(dve, name, j)
                for h in range(4):
                    ins = dve.copy_predicated(PT[:, j // 2, 4 * (j % 2) + h, :], mask,
                                              pa[:, h * P:(h + 1) * P])
                    if h < 3:
                        st.do(ins)
                drain_aux(ins, name, j)

            for j in range(4):
                masked("sc", j, cm)
            for j in range(4):
                wait_aux(dve, "sc", j)
                masked("sx", j, xm)
            for q in range(2):
                hs = slice(4 * q, 4 * q + 4)
                ins = dve.tensor_tensor(pairs(Q[:, hs])[:, :, :, 1, :], pairs(Q[:, hs])[:, :, :, 1, :],
                                        decay(0, q), ALU.mult)
                st.do(ins)
            st.sync()
            dve.tensor_tensor(dec[:, 0], dec[:, 0], dec[:, 1], ALU.mult).then_inc(q2_ready, 1)
            dve.wait_ge(q2_ready, 1)
            wait_stage(dve, "pv", 4)
            o = 16
            st.do(dve.memset(sumA[:, :, 0:o], 0.0))
            st.do(dve.memset(sumB[:, :, 0:o], 0.0))
            st.do(dve.tensor_copy(sumA[:, :, o:o + 1], PV[:, :, 0:1]))
            st.then(dve.tensor_tensor(sumA[:, :, o + 1:], PV[:, :, 1:], PV[:, :, 0:T - 1], ALU.add))
            st.then(dve.tensor_tensor(sumB[:, :, o:], sumA[:, 2:8, o:], sumA[:, 2:8, o - 2:o + T - 2],
                                      ALU.add))
            st.then(dve.tensor_tensor(sumA[:, 4:8, o:], sumB[:, 2:6, o:], sumB[:, 2:6, o - 4:o + T - 4],
                                      ALU.add))
            st.then(dve.tensor_tensor(sumB[:, 4:6, o:], sumA[:, 6:8, o:], sumA[:, 6:8, o - 8:o + T - 8],
                                      ALU.add))
            for g in range(4):
                w = 2 << g
                src = [sumA[:, 0:2], sumB[:, 0:2], sumA[:, 4:6], sumB[:, 4:6]][g]
                invc = C("invc")[:, 16 * g:16 * g + 16]
                st.do(dve.scalar_tensor_tensor(out=PV[:, 2 * g:2 * g + 2, 16:], in0=src[:, :, o + 16:],
                                               scalar=1.0 / w, in1=PV[:, 2 * g:2 * g + 2, 16:],
                                               op0=ALU.mult, op1=ALU.subtract))
                for c in range(2):
                    st.do(dve.tensor_tensor(src[:, c, o:o + 16], src[:, c, o:o + 16], invc, ALU.mult))
                st.sync()
                dve.tensor_tensor(PV[:, 2 * g:2 * g + 2, 0:16], src[:, :, o:o + 16],
                                  PV[:, 2 * g:2 * g + 2, 0:16], ALU.subtract
                                  ).then_inc(pooled_ready, 1)
            def state(c, par, last=False):
                for half in range(2):
                    a = AUX["U"] + half
                    dve.wait_ge(aux_done, c * 2 + (a + 1))
                    hs = slice(4 * half, 4 * half + 4)
                    dve.tensor_tensor(S[:, 1 - par, hs, :], SD[:, hs, :], v3(aux(half), 4), ALU.add
                                      ).then_inc(aux_drained[a % 2], 1)
                if last:
                    return
                for half in range(2):
                    a = AUX["U"] + half
                    dve.wait_ge(aux_drained[a % 2], c + (a // 2 + 1))
                d = DEC[:, bass.ds(c * 2 + 2, 1), :]
                st.then(dve.tensor_tensor(SD[:, :, :], S[:, 1 - par, :, :],
                                          d.rearrange("p a h -> p h a").broadcast_to([P, HEADS, P]),
                                          ALU.mult))

            with st.loop(0, NPAIR // 2 - 1, 2) as i:
                state(i * 2, 0)
                state(i * 2 + 1, 1)
            state(NPAIR - 2, 0, last=True)
            dve.wait_ge(sq_done, 1)
            wait_stage(dve, "og", 4)
            for h in range(HEADS):
                st.do(dve.scalar_tensor_tensor(out=OG[:, h, :], in0=psum[:, 4 + h // 2,
                                               (h % 2) * T:(h % 2 + 1) * T], scalar=V("hg", h),
                                               in1=OG[:, h, :], op0=ALU.mult, op1=ALU.mult))
            for g in range(4):
                lo_of(g, PV[:, 2 * g:2 * g + 2, :], opB, "pooled")
            pa = batch(dve, "osum")
            dve.tensor_scalar(st16[:, :], pa[:, 0:16], 1.0 / P, RMS_EPS, ALU.mult, ALU.add
                              ).then_inc(o_var, 1)
            dve.wait_ge(o_std, 1)
            st.then(dve.reciprocal(st16[:, :], st16[:, :]))
            drain_aux(dve.tensor_tensor(DG[:, :, :], ident.rearrange("p (a b) -> p a b", a=1)
                                        .broadcast_to([P, 16, P]),
                                        st16[:, :].rearrange("p (a b) -> p a b", b=1)
                                        .broadcast_to([P, 16, P]), ALU.mult), "osum")
            wait_aux(dve, "osum")
            dve.tensor_copy(lbd[:, 0:1], st16[:, 0:1]).then_inc(diag_ready, 1)

            def pool_out(j):
                pb = group(dve, "pool", j)
                st.do(dve.scalar_tensor_tensor(out=MB[:, 2 * j, :], in0=pb[:, 0:T], scalar=V("ps", 2 * j),
                                               in1=GB[:, 2 * j, :], op0=ALU.mult, op1=ALU.mult))
                drain(dve.scalar_tensor_tensor(out=MB[:, 2 * j + 1, :], in0=pb[:, T:], scalar=V("ps", 2 * j + 1),
                                               in1=GB[:, 2 * j + 1, :], op0=ALU.mult, op1=ALU.mult),
                      "pool", j)

            def normed(j):
                pa = batch(dve, "obc", j)
                ins = dve.tensor_tensor(OG[:, 2 * j:2 * j + 2, :], OG[:, 2 * j:2 * j + 2, :],
                                        v3(pa, 2), ALU.mult)
                drain_aux(ins, "obc", j)
                wait_aux(dve, "obc", j)
                dve.engine_nop().then_inc(o_ready, 1)

            wait_stage(dve, "gb", 4)
            pool_out(0)
            pool_out(1)
            normed(0)
            normed(1)
            for j in range(2):
                lo_of(j, OG[:, 2 * j:2 * j + 2, :], opC, "o")
            pool_out(2)
            normed(2)
            normed(3)
            for j in range(2, 4):
                lo_of(j, OG[:, 2 * j:2 * j + 2, :], opC, "o")
            pool_out(3)
            dve.wait_ge(mem_sq, 1)
            dve.tensor_scalar(mrs[:, :], mrs[:, :], 1.0 / D, RMS_EPS, ALU.mult, ALU.add
                              ).then_inc(mem_ms, 1)
            dve.wait_ge(mem_sd, 1)
            st.then(dve.reciprocal(mrs[:, :], mrs[:, :]))
            st.do(dve.tensor_scalar(MEM[:, 0, :], MEM[:, 0, :], mrs[:, 0:1], None, ALU.mult))
            dve.tensor_scalar(MEM[:, 1, :], MEM[:, 1, :], mrs[:, 1:2], None, ALU.mult
                              ).then_inc(mem_z, 1)
            wait_stage(dve, "pool", 4)
            for j in range(4):
                pb = group(dve, "wa", j)
                drain(dve.tensor_tensor(AM[:, j], v3(pb, 2), GA[:, 2 * j:2 * j + 2, :], ALU.mult),
                      "wa", j)
                wait_drained(dve, "wa", j)
                dve.tensor_tensor(AM[:, j], AM[:, j], MB[:, 2 * j:2 * j + 2, :], ALU.add
                                  ).then_inc(m_ready, 1)
                lo_of(j, AM[:, j], opA, "m")
            lo_turned("mem", "memT", 0, opB, "memg")
            lo_turned("mem", "memT", 1, opB, "memg")

            def norm(stage, n):
                for j in range(4):
                    if stage == "wo" and j == 2:
                        lo_turned("mem", "memT", 2, opB, "memg")
                        lo_turned("mem", "memT", 3, opB, "memg")
                    pb = group(dve, stage, j)
                    sl = slice(256 * j, 256 * j + 256)
                    drain(dve.scalar_tensor_tensor(out=XR[:, :, sl], in0=XR[:, :, sl], scalar=ALPHA,
                                                   in1=v3(pb, 2), op0=ALU.mult, op1=ALU.add), stage, j)
                    wait_drained(dve, stage, j)
                    for m in range(MT):
                        st.do(dve.bn_stats(bst[:, m, j, :], XR[:, m, sl]))
                st.sync()
                for m in range(MT):
                    st.do(dve.bn_aggr(mv[:, m, :], bst[:, m, :, :]))
                st.sync()
                dve.tensor_scalar(rst[:, :], mv[:, :, 1], LN_EPS, None, ALU.add).then_inc(ln_var, 1)
                if stage == "down":
                    dve.wait_ge(rows_in, 32)
                    for m in range(MT):
                        st.do(dve.scalar_tensor_tensor(
                            out=XR[:, m, :], in0=XR[:, m, :], scalar=mv[:, m, 0:1], in1=LNR[:, 0, :],
                            op0=ALU.subtract, op1=ALU.mult))
                dve.wait_ge(ln_std, n)
                st.then(dve.reciprocal(rst[:, :], rst[:, :]))
                if stage == "down":
                    for m in range(MT):
                        dve.scalar_tensor_tensor(
                            out=XR[:, m, :], in0=XR[:, m, :], scalar=rst[:, m:m + 1], in1=LNR[:, 1, :],
                            op0=ALU.mult, op1=ALU.add).then_inc(x_new, 1)
                    return
                for m in range(MT):
                    ins = dve.tensor_scalar(XR[:, m, :], XR[:, m, :], mv[:, m, 0:1], rst[:, m:m + 1],
                                            ALU.subtract, ALU.mult)
                    if m == 0:
                        st.do(ins)
                ins.then_inc(ln_z, 1)
                dve.wait_ge(ln_z, n)

            def gain_and_bias(done):
                for m in range(MT):
                    st.then(dve.tensor_tensor(XR[:, m, :], XR[:, m, :], LNR[:, 0, :], ALU.mult))
                    dve.tensor_tensor(XR[:, m, :], XR[:, m, :], LNR[:, 1, :], ALU.add
                                      ).then_inc(done, 1)

            dve.wait_ge(xr_in, 16)
            norm("wo", 1)
            for j in range(4):
                pa = batch(dve, "ln1T", j)
                if j >= 2:
                    has_lo(dve, "ln1", j - 2)
                for c in (2 * j, 2 * j + 1):
                    ins = dve.tensor_scalar(LT[:, j % 2, c % 2, :], pa[:, (c % 2) * T:(c % 2 + 1) * T],
                                            V("ln1g", c), V("ln1b", c), ALU.mult, ALU.add)
                    if c % 2 == 0:
                        st.do(ins)
                drain_aux(ins, "ln1T", j)
                wait_aux(dve, "ln1T", j)
                dve.engine_nop().then_inc(ln_op, 1)
                if j % 2:
                    lo_of(j - 1, LT[:, 0], opC, "ln1")
                    lo_of(j, LT[:, 1], opC, "ln1")
            dve.wait_ge(rows_in, 16)
            gain_and_bias(x_res)
            with st.loop(0, 4, 4) as i:
                for s in range(4):
                    dve.wait_ge(split_hi, i * 4 + (SPLIT["h"] + s + 1))
                    dve.wait_ge(split_lo, i * 4 + (SPLIT["h"] + s))
                    st.then(dve.tensor_tensor(RQ[:, s % 2], RL[:, s % 2], RL[:, s % 2], ALU.mult))
                    cs = bass.ds(i * 8 + 2 * s, 2)
                    dve.tensor_tensor(HT[1][:, cs, :], RQ[:, s % 2], HT[0][:, cs, :], ALU.subtract
                                      ).then_inc(split_lo, 1)
            dve.wait_ge(x_res, 2)
            norm("down", 2)

            def rms(n):
                dve.wait_ge(rms_sq, n)
                if n > 1:
                    st.then(dve.tensor_reduce(rst[:, :], ssq[:, :, :], AX, ALU.add))
                dve.tensor_scalar(rst[:, :], ssq[:, :, 0] if n == 1 else rst[:, :], 1.0 / D, RMS_EPS,
                                  ALU.mult, ALU.add).then_inc(rms_ms, 1)
                dve.wait_ge(rms_sd, n)
                dve.reciprocal(rst[:, :], rst[:, :]).then_inc(rms_rst, 1)
                dve.wait_ge(rms_rst, n)

            def rms_across(n, name, gain, op):
                rms(n)
                dve.tensor_scalar(XN[:, 0, :], XR[:, 0, :], rst[:, 0:1], None, ALU.mult
                                  ).then_inc(rms_z, 1)
                for j in range(4):
                    lo_turned(name[:2], name, j, op, gain)

            rms_across(1, "h2T", "mixg", opC)
            cos, sin = (C(n).rearrange("p (a t) -> p a t", a=1).broadcast_to([P, 2, T])
                        for n in ("cos", "sin"))
            for stage, dst in (("q2", QR), ("k2", KR)):
                for j in range(2):
                    pb = group(dve, stage, j)
                    st.do(dve.tensor_tensor(R1[:, :, :], v3(pb, 2), cos, ALU.mult))
                    st.then(dve.tensor_tensor(R2[:, :, :], v3(pb, 2), sin, ALU.mult))
                    st.do(dve.tensor_tensor(dst[:, j, 0, :], R1[:, 0, :], R2[:, 1, :], ALU.subtract))
                    drain(dve.tensor_tensor(dst[:, j, 1, :], R1[:, 1, :], R2[:, 0, :], ALU.add), stage, j)
                    wait_drained(dve, stage, j)

            def att_softmax(a):
                dve.wait_ge(quad_done, 2 * a + 1)
                st.then(dve.scalar_tensor_tensor(
                    out=AS[:, :, :], in0=psum[:, 4:8, 0:384], scalar=float(MHD) ** -0.5,
                    in1=C("amask").rearrange("p (a b) -> p a b", a=1).broadcast_to([P, 4, 384]),
                    op0=ALU.mult, op1=ALU.add))
                am = amx[:, :].rearrange("p (h m) -> p h m", m=2)
                st.do(dve.tensor_reduce(am[:, :, 0], AS[:, :, 0:P], AX, ALU.max))
                st.then(dve.tensor_reduce(am[:, :, 1], AS[:, :, P:3 * P], AX, ALU.max))
                dve.tensor_scalar(amx[:, :], amx[:, :], -1.0, None, ALU.mult).then_inc(att_max, 1)

            def att_weights(a):
                dve.wait_ge(att_exp, a + 1)
                st.then(dve.reciprocal(asm[:, :], asm[:, :]))
                sm = asm[:, :].rearrange("p (h m) -> p h m", m=2)
                st.do(dve.tensor_tensor(AS[:, :, 0:P], AS[:, :, 0:P],
                                        sm[:, :, 0:1].broadcast_to([P, 4, P]), ALU.mult))
                dve.tensor_tensor(AS[:, :, P:3 * P], AS[:, :, P:3 * P],
                                  sm[:, :, 1:2].broadcast_to([P, 4, 2 * P]), ALU.mult
                                  ).then_inc(att_p, 1)

            att_softmax(0)
            dve.engine_nop().then_inc(quad_read, 1)
            att_weights(0)
            dve.wait_ge(att_t, 1)
            dve.engine_nop().then_inc(quad_read, 1)
            att_softmax(1)
            att_weights(1)

            def att_out(a):
                pa = batch(dve, f"pv{a}")
                drain_aux(lower(a, v3(pa, 2), AT, "at"), f"pv{a}")
                lo_drained("at", f"pv{a}", 0)

            att_out(0)
            dve.wait_ge(gv_sq, 1)
            dve.tensor_scalar(ssq[:, :, 2], ssq[:, :, 1], 1.0 / 512, RMS_EPS, ALU.mult, ALU.add
                              ).then_inc(gv_ms, 1)
            dve.wait_ge(gv_sd, 1)
            st.then(dve.reciprocal(ssq[:, :, 3], ssq[:, :, 2]))
            dve.wait_ge(gml_in, 64)
            for m in range(MT):
                dve.scalar_tensor_tensor(out=GV[:, m, :], in0=GV[:, m, :], scalar=ssq[:, m, 3:4],
                                         in1=GR[:, :], op0=ALU.mult, op1=ALU.mult).then_inc(gv_n, 1)
            att_out(1)
            for n in range(2):
                pa = batch(dve, "z", n)
                bs = BS[:, 2 * n:2 * n + 2, :]
                for m in range(MT):
                    ins = dve.tensor_tensor(
                        ZB[:, n, :, m, :], pa.rearrange("p (c m t) -> p c m t", c=2, m=MT)[:, :, m, :],
                        bs, ALU.add)
                    if m == 0:
                        st.do(ins)
                drain_aux(ins, "z", n)
                wait_aux(dve, "z", n)
                zb = ZB[:, n].rearrange("p c m t -> p c (m t)")
                dve.tensor_tensor(zb, zb, GU[:, 2 * n:2 * n + 2, :], ALU.mult).then_inc(gm_ready, 1)
                lo_of(n, zb, GM, "gm")
            wait_stage(dve, "gb2", 4)
            for j in range(4):
                pb = group(dve, "ma", j)
                drain(dve.tensor_tensor(MA[:, 2 * j:2 * j + 2, :], v3(pb, 2),
                                        GA2[:, 2 * j:2 * j + 2, :], ALU.mult), "ma", j)
            wait_stage(dve, "ma", 4)
            for j in range(4):
                pb = group(dve, "gm", j)
                drain(dve.tensor_tensor(AM[:, j], v3(pb, 2), GB2[:, 2 * j:2 * j + 2, :], ALU.mult),
                      "gm", j)
                wait_drained(dve, "gm", j)
                dve.tensor_tensor(AM[:, j], AM[:, j], MA[:, 2 * j:2 * j + 2, :], ALU.add
                                  ).then_inc(m2_ready, 1)
                lo_of(j, AM[:, j], opC, "m2")

            def residual(stage):
                for j in range(4):
                    pb = group(dve, stage, j)
                    sl = slice(256 * j, 256 * j + 256)
                    drain(dve.tensor_tensor(XR[:, :, sl], XR[:, :, sl], v3(pb, 2), ALU.add), stage, j)
                    wait_drained(dve, stage, j)
                    dve.engine_nop().then_inc(x_new, 1)

            residual("wo2")
            rms_across(2, "h3T", "xag", opB)
            for n in range(2):
                cs = slice(4 * n, 4 * n + 4)
                dve.wait_ge(quad_done, 5 + n)
                st.then(dve.tensor_reduce(amx[:, cs].rearrange("p (h m) -> p h m", m=2),
                                          psum[:, 4 + 2 * n:6 + 2 * n, :].rearrange(
                                              "p h (m t) -> p h m t", m=2), AX, ALU.max))
                dve.tensor_scalar(amx[:, cs], amx[:, cs], -float(XHD) ** -0.5, None, ALU.mult
                                  ).then_inc(att_max, 1)
            for n in range(2):
                cs = slice(4 * n, 4 * n + 4)
                dve.wait_ge(att_exp, 3 + n)
                st.then(dve.reciprocal(asm[:, cs], asm[:, cs]))
                dve.tensor_tensor(XS[:, cs, :], XS[:, cs, :], asm[:, cs].rearrange(
                    "p (a b) -> p a b", b=1).broadcast_to([P, 4, T]), ALU.mult).then_inc(att_p, 1)
            for n in range(2):
                lo_turned("ax", "xpv", n, AXo)
            residual("xo")
            rms_across(3, "h4T", "ffng", opB)
            dve.wait_ge(rows2_in, 16)
            for m in range(MT):
                st.do(dve.tensor_tensor(XN[:, m, :], XN[:, m, :], LNR[:, 0, :], ALU.mult))

            TOP_STEPS = [0]

            def top16(lists):
                for vals, idx, src, work in lists:
                    st.do(dve.max(vals[:, 0:8], src))
                st.sync()
                for vals, idx, src, work in lists:
                    st.do(dve.match_replace(work, vals[:, 0:8], src, LOWEST))
                st.sync()
                for vals, idx, src, work in lists:
                    st.do(dve.max(vals[:, 8:16], work))
                    st.do(dve.max_index(idx[:, 0:8], vals[:, 0:8], src))
                st.sync()
                for vals, idx, src, work in lists:
                    st.do(dve.max_index(idx[:, 8:16], vals[:, 8:16], work))
                st.sync()

            def topk(it):
                n0, st.met = st.n, (small_in, 16)
                sc = SC[:, :, :, :].rearrange("p m (h q) n -> p (m h) (q n)", q=2)
                src = sc[:, it, :] if isinstance(it, int) else \
                    sc[:, bass.ds(it, 1), :].rearrange("p a b -> p (a b)")
                st.then(dve.tensor_copy(sS[:, :, :].rearrange("p a b -> p (a b)"), src))
                top16([(tv[:, q, :], ti[:, q, :], sS[:, q, :], sW[:, q * NK:(q + 1) * NK])
                       for q in range(2)])
                st.then(dve.tensor_copy(tif[:, :, :], ti[:, :, :]))
                b16 = [P, 16, 16]
                col = lambda ap: ap.rearrange("p (a b) -> p a b", b=1).broadcast_to(b16)
                row = lambda ap: ap.rearrange("p (a b) -> p a b", a=1).broadcast_to(b16)
                st.then(dve.tensor_tensor(cand[:, :, :], col(tv[:, 0, :]), row(tv[:, 1, :]), ALU.add))
                top16([(cv[:, :], cp[:, 0, :], cand[:, :, :].rearrange("p a b -> p (a b)"), sW[:, :])])
                dve.tensor_scalar(gs[:, 0:1], cv[:, 0:1], -1.0, None, ALU.mult).then_inc(top_v, 1)
                st.then(dve.tensor_scalar(cp[:, 1, :], cp[:, 0, :], 15, None, ALU.bitwise_and))
                st.then(dve.tensor_scalar(cp[:, 0, :], cp[:, 0, :], 4, None, ALU.logical_shift_right))
                st.then(dve.tensor_copy(cpf[:, :, :], cp[:, :, :]))
                b32 = [P, 32, 16]
                eq3 = eq[:, :, :, :].rearrange("p q a b -> p (q a) b")
                st.then(dve.tensor_tensor(
                    eq3, C("iota").rearrange("p (a b) -> p a b", a=1).broadcast_to(b32),
                    cpf[:, :, :].rearrange("p q (a b) -> p (q a) b", b=1).broadcast_to(b32), ALU.is_equal))
                st.then(dve.tensor_tensor(
                    eq[:, :, :, :], eq[:, :, :, :], tif[:, :, :].rearrange("p q (a b) -> p q a b", a=1)
                    .broadcast_to([P, 2, 16, 16]), ALU.mult))
                st.then(dve.tensor_reduce(ef[:, :, :].rearrange("p q a -> p (q a)"), eq3, AX, ALU.add))
                dst = IDX[:, it, :] if isinstance(it, int) else \
                    IDX[:, bass.ds(it, 1), :].rearrange("p a b -> p (a b)")
                dve.scalar_tensor_tensor(out=dst, in0=ef[:, 0, :], scalar=float(NK), in1=ef[:, 1, :],
                                         op0=ALU.mult, op1=ALU.add).then_inc(idx_ready, 1)
                dve.wait_ge(top_e, it + 1)
                st.then(dve.reciprocal(gs[:, 1:2], gs[:, 1:2]))
                gdst = GW[:, it, :] if isinstance(it, int) else \
                    GW[:, bass.ds(it, 1), :].rearrange("p a b -> p (a b)")
                st.then(dve.tensor_scalar(gdst, gx[:, :], gs[:, 1:2], None, ALU.mult))
                TOP_STEPS[0], st.met = st.n - n0, None

            wait_aux(dve, "psc", 0)
            topk(0)
            per_topk = TOP_STEPS[0]

            def pass_(m, it, par):
                if not (isinstance(it, int) and it == 15):
                    topk(it + 1)
                for k in range(TOPK):
                    dve.wait_ge(rd_in[k % 8], it * 32 + 16 * (k // 8 + 1))
                    dve.tensor_tensor_reduce(
                        out=JUNK[:, :], in0=RD[k % 8][:, :], in1=XN[:, m, :], scale=1.0,
                        scalar=0.0, op0=ALU.mult, op1=ALU.add,
                        accum_out=dots[:, par, k:k + 1]).then_inc(dot_done, 1)
                    dve.wait_ge(dot_done, it * 16 + (k + 1))
                dve.wait_ge(gelu_done, it + 1)
                gate = GW[:, it, :] if isinstance(it, int) else \
                    GW[:, bass.ds(it, 1), :].rearrange("p a b -> p (a b)")
                dve.tensor_tensor(coef[:, par, :], act_d[:, par, :], gate, ALU.mult
                                  ).then_inc(coef_ready, 1)

            wait_aux(dve, "psc", 1)
            pass_(0, 0, 0)
            wait_aux(dve, "psc", 2)
            pass_(0, 1, 1)
            wait_aux(dve, "psc", 6)
            wait_aux(dve, "psc", 7)
            for m, first, trips in ((0, 2, 3), (1, 8, 3)):
                with st.loop(0, trips, 2 * per_topk) as i:
                    for par in range(2):
                        pass_(m, i * 2 + (first + par), par)

            def last_norm(m):
                dve.wait_ge(up_done, 128 * (m + 1) - m * len(BY_DVE))
                dve.tensor_tensor(XR[:, m, :], XR[:, m, :],
                                  psum[:, 4 + 2 * m:6 + 2 * m, :].rearrange("p a b -> p (a b)"),
                                  ALU.add).then_inc(fin_x, 1)
                dve.wait_ge(fin_sq, m + 1)
                dve.tensor_scalar(rst[:, m:m + 1], ssq[:, m, 0:1], 1.0 / D, RMS_EPS, ALU.mult, ALU.add
                                  ).then_inc(fin_ms, 1)
                dve.wait_ge(fin_sd, m + 1)
                st.then(dve.reciprocal(rst[:, m:m + 1], rst[:, m:m + 1]))
                dve.scalar_tensor_tensor(out=YO[:, m, :], in0=XR[:, m, :], scalar=rst[:, m:m + 1],
                                         in1=LNR[:, 1, :], op0=ALU.mult, op1=ALU.mult
                                         ).then_inc(fin_y, 1)

            pass_(1, 14, 0)
            pass_(1, 15, 1)
            last_norm(0)
            for k in BY_DVE:
                dve.wait_ge(ru_in[k % 8], 15 * 32 + 16 * (k // 8 + 1))
                st.then(dve.scalar_tensor_tensor(out=XR[:, 1, :], in0=RU[k % 8][:, :],
                                                 scalar=coef[:, 1, k:k + 1], in1=XR[:, 1, :],
                                                 op0=ALU.mult, op1=ALU.add))
            last_norm(1)

        @block.gpsimd
        def _(pool):
            def lower_part(s, ready, first=False):
                for h in (1,) if first else (0, 1):
                    if first:
                        pool.wait_ge(lo_ready, 1)
                    ks = slice(4 * h, 4 * h + 4)
                    pool.wait_ge(hi_ready, ready + h)
                    pool.tensor_tensor(w_lo[s][:, ks, :], raw[s][:, ks, :], w_hi[s][:, ks, :],
                                       ALU.subtract).then_inc(lo_ready, 1)

            cut = BLOCK["ga2"] // 4 + 1
            for b in range(4):
                lower_part(b, half_end(b, 0), b == 0)
            with pool.Fori(1, cut) as i:
                for s in range(4):
                    lower_part(s, i * 8 + half_end(s, 0))
            pool.wait_ge(gml_in, 64)
            pool.affine_select(out=WS[:, :, :], in_=WS[:, :, :], compare_op=ALU.is_ge, fill=0.0, base=0,
                               pattern=[[0, 8], [1, P]], channel_multiplier=-1).then_inc(ws_masked, 1)
            with pool.Fori(cut, NBLOCKS // 4 - 1) as i:
                for s in range(4):
                    lower_part(s, i * 8 + half_end(s, 0))
            tail = list(range(NBLOCKS // 4 * 4 - 4, NBLOCKS))
            while len(tail) > 2:
                b = tail.pop(0)
                lower_part(b % 4, half_end(b, 0))

            st = Steps(pool, pool_step)

            st.met = (gemm_done, 2 * NBLOCKS)

            def take_indices(it, par):
                src = IDX[:, it, :] if isinstance(it, int) else \
                    IDX[:, bass.ds(it, 1), :].rearrange("p a b -> p (a b)")
                pool.wait_ge(idx_ready, it + 1)
                st.then(pool.tensor_copy(cur[:, par, :], src))

            def gather(dst, table, par, k, ready):
                pool.indirect_dma_start(
                    out=dst[:, :], out_offset=None, in_=table,
                    in_offset=bass.IndirectOffsetOnAxis(ap=cur[:, par, k:k + 1], axis=0)
                ).then_inc(ready, 16)

            def down_rows(it, par, k):
                if not (isinstance(it, int) and it == 0 and k < 8):
                    st.wait(dot_done, it * 16 + (k - 7))
                gather(RD[k % 8], w_down, par, k, rd_in[k % 8])

            def up_rows(it, par, k):
                if isinstance(it, int) and it == 0 and k < 8:
                    pool.wait_ge(gemm_done, half_end(RU_AFTER[k // 2]))
                else:
                    st.wait(up_done, it * 16 + (k - 7))
                gather(RU[k % 8], w_up, par, k, ru_in[k % 8])

            def both(it, par):
                take_indices(it + 1, (par + 1) % 3)
                for k in range(TOPK):
                    down_rows(it + 1, (par + 1) % 3, k)
                    up_rows(it, par, k)

            take_indices(0, 0)
            for k in range(TOPK):
                down_rows(0, 0, k)
                if k in (7, 11):
                    b = tail.pop(0)
                    lower_part(b % 4, half_end(b, 0))
            both(0, 0)
            with st.loop(0, 4, 3) as i:
                both(i * 3 + 1, 1)
                both(i * 3 + 2, 2)
                both(i * 3 + 3, 0)
            both(13, 1)
            both(14, 2)
            for k in range(TOPK):
                up_rows(15, 0, k)


def kernel(**inputs):
    import concourse.bacc as bacc
    from concourse.bass_utils import run_bass_kernel_spmd as run

    a = {k: np.asarray(v) for k, v in inputs.items()}

    def k1024(w):
        c = w.shape[1] // 256
        return w.reshape(8, P, c, 256).transpose(2, 1, 0, 3).reshape(c, P, 2048)

    def k512(w):
        return w.reshape(4, P, 2, 2, 256).transpose(2, 1, 3, 0, 4).reshape(2, P, 2048)

    w_in = a["w_in"][0]
    c = lambda n: slice(n * 1024, (n + 1) * 1024)
    q_, f_, i_, og_, pv_, ga_, gb_ = (w_in[:, c(n)] for n in range(7))
    w2 = a["w_in_2"][0]
    order = np.arange(512).reshape(2, 4, 2, 32).transpose(0, 2, 1, 3).reshape(-1)
    pieces = [
        k1024(f_), k1024(q_), k1024(i_), k1024(pv_), k1024(og_), k1024(ga_), k1024(gb_),
        a["w_pool"][0].reshape(4, 2, P, 256).transpose(2, 0, 1, 3).reshape(1, P, 2048),
        k1024(a["w_a"][0]), k1024(a["w_out"][0]), k1024(a["xa_w_kv_2"][0][:, :256]),
        k1024(a["w_up"][0]),
        a["w_down"][0].reshape(4, 8, P, 4, 256).transpose(3, 0, 2, 1, 4).reshape(16, P, 2048),
        k1024(a["xa_w_kv_2"][0][:, 512:]),
        k1024(w2[:, 0:512][:, order]), k1024(w2[:, 512:1024][:, order]), k1024(w2[:, 1024:1536]),
        k1024(w2[:, 1536:2048]), k1024(w2[:, 2048:2560]), k1024(w2[:, 2560:3584]),
        k1024(w2[:, 3584:4608]), k512(a["moba_w_proj_2"][0]), k512(a["gmlp_w_proj_2"][0]),
        k1024(a["w_out_2"][0]), k1024(a["xa_w_kv_2"][0][:, 256:512]), k1024(a["xa_w_q_2"][0]), k512(a["xa_w_o_2"][0]),
        k1024(a["peer_w_q_2"][0]),
    ]
    weights = np.concatenate(pieces)
    assert weights.shape[0] == NBLOCKS
    col = lambda v: v.reshape(8, P).T
    vecs = np.concatenate([col(v) for v in (
        a["lb_logits"][0], a["lb_logits"][1], a["hgrn_norm_g"][0], a["pool_scale"][0], a["ln1_g"][0],
        a["ln1_b"][0], a["norm_mix_g_2"][0], a["norm_xa_g_2"][0], a["norm_mem_g_2"][0],
        a["norm_ffn_g_2"][0])], axis=1)

    s, t = np.arange(P)[:, None], np.arange(P)[None, :]
    con = np.zeros((P, NCON), np.float32)

    def put(n, v):
        o, k = CON[n]
        con[:, o:o + k] = v

    put("ident", np.eye(P))
    put("ones", 1.0)
    causal = np.where(t <= s, 0.0, NEG)
    put("amask", np.concatenate([causal, np.zeros((P, P)), causal], axis=1))
    put("cmask", ((s // CH == t // CH) & (s <= t)).astype(np.float32))
    freq = np.float32(10000.0) ** (-np.arange(32, dtype=np.float32) / np.float32(32))
    ang = np.arange(T, dtype=np.float32)[None, :] * freq[np.arange(P) % 32][:, None]
    put("cos", np.cos(ang.astype(np.float32)))
    put("sin", np.sin(ang.astype(np.float32)))
    put("invc", np.concatenate([1.0 / np.minimum(np.arange(16) + 1, 2 << g) for g in range(4)])[None])
    put("reset", (np.arange(T) % CH != 0).astype(np.float32)[None])
    put("xmask", ((s // PAIR == t // PAIR) & (s // CH < t // CH)).astype(np.float32))
    put("iota", np.arange(16)[None])

    pad = np.zeros(512, np.float32)
    rows = np.stack([a["ln1_g"][0], a["ln1_b"][0], a["ln2_g"][0], a["ln2_b"][0],
                     np.concatenate([a["gmlp_norm_g_2"][0], pad]), a["norm_ffn_g_2"][0], a["final_g_2"]])
    arrays = {
        "weights": weights, "vecs": vecs, "consts": con,
        "xT": a["x"][0].T.reshape(8, P, T).transpose(1, 0, 2), "x": a["x"][0], "mem": a["mem_2"][0],
        "rows": rows, "gws": a["gmlp_w_s_2"][0].transpose(2, 0, 1),
        "gbs": a["gmlp_b_s_2"][0].reshape(4, 2, P).transpose(1, 0, 2),
        "subkeys": a["peer_subkeys_2"][0].reshape(16, NK, P).transpose(2, 0, 1),
        "w_down": a["peer_w_down_2"][0], "w_up": a["peer_w_up_2"][0],
    }
    arrays = {k: np.ascontiguousarray(v) for k, v in arrays.items()}
    nc = bacc.Bacc("TRN2", target_bir_lowering=False, num_devices=1)
    args = [nc.dram_tensor(k, v.shape, F32, kind="ExternalInput").ap() for k, v in arrays.items()]
    args.append(nc.dram_tensor("out", (T, D), F32, kind="ExternalOutput").ap())
    build(nc, *args)
    r = run(nc, [arrays], core_ids=[0])
    return r.results[0]["out"].reshape(1, T, D)
```
